# Optimizing a Trainium2 kernel written in Bass

```python
import math
import jax, jax.numpy as jnp
from jax import lax
import numpy as np
import jax
import jax.numpy as jnp

D_MODEL = 2048
BATCH = 1
SEQ = 256
DEPTH = 1

CHUNK = 64
N_META = 16
Q_BLOCK = 128
EPS = 1e-6

D_SSM = D_MODEL // 2
SSM_GROUP = 16
N_SSM_GROUPS = D_SSM // SSM_GROUP
SSM_STATE = 64
DT_MIN = 1e-3
DT_MAX = 1e-1

MLA_HEADS = 8
QK_NOPE = 128
QK_ROPE = 64
V_HEAD = 128
Q_LORA = 512
KV_LORA = 256
D_ATTN = MLA_HEADS * V_HEAD
ROPE_BASE = 10000.0

D_MIX = D_SSM + D_ATTN
D_IN = D_SSM + Q_LORA + KV_LORA + QK_ROPE

D_FF = 5504
CONV_W = 3


def rmsnorm(x, g):
    xf = x.astype(jnp.float32)
    y = xf * lax.rsqrt(jnp.mean(xf * xf, axis=-1, keepdims=True) + EPS)
    return (y * g.astype(jnp.float32)).astype(x.dtype)

def rotary(x, cos, sin):
    x1, x2 = jnp.split(x, 2, axis=-1)
    return jnp.concatenate([x1 * cos - x2 * sin, x2 * cos + x1 * sin], axis=-1)

def s5_mixer(u, lam_re, lam_im, log_dt, b_re, b_im, c_re, c_im, d_skip, w_glu, b_glu):
    bsz, L, _ = u.shape
    f32 = jnp.float32
    uf = u.astype(f32).reshape(bsz, L, N_SSM_GROUPS, SSM_GROUP)
    lam = lax.complex(lam_re.astype(f32), lam_im.astype(f32))
    dt = jnp.exp(log_dt.astype(f32))[:, None]
    lam_bar = jnp.exp(lam * dt)
    b = lax.complex(b_re.astype(f32), b_im.astype(f32))
    b_bar = ((lam_bar - 1.0) / lam)[..., None] * b
    bu = jnp.einsum('blgc,gpc->blgp', uf.astype(jnp.complex64), b_bar)
    a = jnp.broadcast_to(lam_bar, bu.shape)

    def combine(e1, e2):
        a1, s1 = e1
        a2, s2 = e2
        return a1 * a2, a2 * s1 + s2

    _, h = lax.associative_scan(combine, (a, bu), axis=1)
    c = lax.complex(c_re.astype(f32), c_im.astype(f32))
    y = jnp.real(jnp.einsum('blgp,gcp->blgc', h, c))
    y = y + d_skip.astype(f32).reshape(N_SSM_GROUPS, SSM_GROUP) * uf
    y = y.reshape(bsz, L, D_SSM)
    g = jax.nn.gelu(y)
    out = g * jax.nn.sigmoid(g @ w_glu.astype(f32) + b_glu.astype(f32))
    return out.astype(u.dtype)

def mla_mixer(q_a, kv_a, k_pe, q_a_norm, w_q_b, kv_a_norm, w_kv_b, cos, sin, chunk_id):
    bsz, L, _ = q_a.shape
    q = (rmsnorm(q_a, q_a_norm) @ w_q_b).reshape(bsz, L, MLA_HEADS, QK_NOPE + QK_ROPE)
    q_nope, q_pe = q[..., :QK_NOPE], q[..., QK_NOPE:]
    q_pe = rotary(q_pe, cos[:, None, :], sin[:, None, :])
    kv = (rmsnorm(kv_a, kv_a_norm) @ w_kv_b).reshape(bsz, L, MLA_HEADS, QK_NOPE + V_HEAD)
    k_nope, v = kv[..., :QK_NOPE], kv[..., QK_NOPE:]
    k_pe = rotary(k_pe, cos, sin)
    scale = 1.0 / math.sqrt(QK_NOPE + QK_ROPE)

    n_blk = -(-L // Q_BLOCK)
    pad = n_blk * Q_BLOCK - L

    def to_blocks(t):
        t = jnp.pad(t, ((0, 0), (0, pad)) + ((0, 0),) * (t.ndim - 2))
        return jnp.moveaxis(t.reshape(bsz, n_blk, Q_BLOCK, *t.shape[2:]), 1, 0)

    q_cid = jnp.pad(chunk_id, (0, pad), constant_values=2 ** 30).reshape(n_blk, Q_BLOCK)

    def attend(args):
        qn, qp, qc = args
        s = jnp.einsum('bqhd,bkhd->bhqk', qn, k_nope, preferred_element_type=jnp.float32)
        s = s + jnp.einsum('bqhr,bkr->bhqk', qp, k_pe, preferred_element_type=jnp.float32)
        mask = chunk_id[None, :] <= qc[:, None]
        s = jnp.where(mask[None, None], s * scale, jnp.finfo(jnp.float32).min)
        p = jax.nn.softmax(s, axis=-1).astype(v.dtype)
        return jnp.einsum('bhqk,bkhd->bqhd', p, v)

    o = lax.map(attend, (to_blocks(q_nope), to_blocks(q_pe), q_cid))
    o = jnp.moveaxis(o, 0, 1).reshape(bsz, n_blk * Q_BLOCK, D_ATTN)[:, :L]
    return o

def conv_ffn(x, w_up, conv_w, conv_b, w_down):
    L = x.shape[1]
    gate, val = jnp.split(x @ w_up, 2, axis=-1)
    gp = jnp.pad(gate, ((0, 0), (CONV_W - 1, 0), (0, 0)))
    gate = sum(conv_w[k] * gp[:, k:k + L] for k in range(CONV_W)) + conv_b
    return (jax.nn.silu(gate) * val) @ w_down

def first_inputs(seed: int = 0) -> dict:
    key = jax.random.key(seed)
    ks = jax.random.split(key, 32)
    f32 = jnp.float32
    nrm = lambda k, shape, s: jax.random.normal(k, shape, f32) * s
    gain = lambda k, shape: 1.0 + 0.01 * jax.random.normal(k, shape, f32)
    G, P, C = N_SSM_GROUPS, SSM_STATE, SSM_GROUP
    lam_re = -0.5 + 0.01 * jax.random.normal(ks[4], (DEPTH, G, P), f32)
    lam_im = jnp.pi * jnp.arange(P, dtype=f32)[None, None, :] + 0.01 * jax.random.normal(ks[5], (DEPTH, G, P), f32)
    log_dt = jax.random.uniform(ks[6], (DEPTH, G), f32, math.log(DT_MIN), math.log(DT_MAX))
    return {
        "x": jax.random.normal(ks[0], (BATCH, SEQ, D_MODEL), f32),
        "meta_tokens": nrm(ks[1], (N_META, D_MODEL), 1.0),
        "mix_norm": gain(ks[2], (DEPTH, D_MODEL)),
        "w_in": nrm(ks[3], (DEPTH, D_MODEL, D_IN), D_MODEL ** -0.5),
        "lam_re": lam_re,
        "lam_im": lam_im,
        "log_dt": log_dt,
        "b_re": nrm(ks[7], (DEPTH, G, P, C), (2 * C) ** -0.5),
        "b_im": nrm(ks[8], (DEPTH, G, P, C), (2 * C) ** -0.5),
        "c_re": nrm(ks[9], (DEPTH, G, C, P), (2 * P) ** -0.5),
        "c_im": nrm(ks[10], (DEPTH, G, C, P), (2 * P) ** -0.5),
        "d_skip": nrm(ks[11], (DEPTH, D_SSM), 1.0),
        "w_glu": nrm(ks[12], (DEPTH, D_SSM, D_SSM), D_SSM ** -0.5),
        "b_glu": nrm(ks[13], (DEPTH, D_SSM), 0.01),
        "q_a_norm": gain(ks[14], (DEPTH, Q_LORA)),
        "w_q_b": nrm(ks[15], (DEPTH, Q_LORA, MLA_HEADS * (QK_NOPE + QK_ROPE)), Q_LORA ** -0.5),
        "kv_a_norm": gain(ks[16], (DEPTH, KV_LORA)),
        "w_kv_b": nrm(ks[17], (DEPTH, KV_LORA, MLA_HEADS * (QK_NOPE + V_HEAD)), KV_LORA ** -0.5),
        "out_norm_ssm": gain(ks[18], (DEPTH, D_SSM)),
        "out_norm_attn": gain(ks[19], (DEPTH, D_ATTN)),
        "w_out": nrm(ks[20], (DEPTH, D_MIX, D_MODEL), D_MIX ** -0.5),
        "ffn_norm": gain(ks[21], (DEPTH, D_MODEL)),
        "w_up": nrm(ks[22], (DEPTH, D_MODEL, 2 * D_FF), D_MODEL ** -0.5),
        "conv_w": nrm(ks[23], (DEPTH, CONV_W, D_FF), CONV_W ** -0.5),
        "conv_b": nrm(ks[24], (DEPTH, D_FF), 0.01),
        "w_down": nrm(ks[25], (DEPTH, D_FF, D_MODEL), D_FF ** -0.5),
        "final_norm": gain(ks[26], (D_MODEL,)),
    }

def first_block(x, meta_tokens, mix_norm, w_in, lam_re, lam_im, log_dt, b_re, b_im, c_re, c_im,
              d_skip, w_glu, b_glu, q_a_norm, w_q_b, kv_a_norm, w_kv_b, out_norm_ssm,
              out_norm_attn, w_out, ffn_norm, w_up, conv_w, conv_b, w_down, final_norm):
    bsz = x.shape[0]
    meta = jnp.broadcast_to(meta_tokens.astype(x.dtype)[None], (bsz, N_META, D_MODEL))
    h = jnp.concatenate([meta, x], axis=1)
    L = h.shape[1]

    pos = jnp.arange(L, dtype=jnp.int32)
    chunk_id = jnp.where(pos < N_META, 0, 1 + (pos - N_META) // CHUNK)
    inv_freq = 1.0 / (ROPE_BASE ** (jnp.arange(0, QK_ROPE, 2, dtype=jnp.float32) / QK_ROPE))
    ang = pos.astype(jnp.float32)[:, None] * inv_freq[None, :]
    cos = jnp.cos(ang).astype(x.dtype)
    sin = jnp.sin(ang).astype(x.dtype)

    for i in range(DEPTH):
        xn = rmsnorm(h, mix_norm[i])
        z = xn @ w_in[i]
        o1 = D_SSM
        o2 = o1 + Q_LORA
        o3 = o2 + KV_LORA
        u, q_a, kv_a, k_pe = z[..., :o1], z[..., o1:o2], z[..., o2:o3], z[..., o3:]
        ya = s5_mixer(u, lam_re[i], lam_im[i], log_dt[i], b_re[i], b_im[i], c_re[i], c_im[i],
                      d_skip[i], w_glu[i], b_glu[i])
        yb = mla_mixer(q_a, kv_a, k_pe, q_a_norm[i], w_q_b[i], kv_a_norm[i], w_kv_b[i],
                       cos, sin, chunk_id)
        y = jnp.concatenate([rmsnorm(ya, out_norm_ssm[i]), rmsnorm(yb, out_norm_attn[i])], axis=-1)
        h = h + y @ w_out[i]
        h = h + conv_ffn(rmsnorm(h, ffn_norm[i]), w_up[i], conv_w[i], conv_b[i], w_down[i])

    return rmsnorm(h, final_norm)[:, N_META:]


_first_inputs = first_inputs


def first_inputs(seed=0):
    import zlib

    import numpy as np

    out = dict(_first_inputs(seed))
    spreads = {}
    factors = {'mix_norm': 5.232,
     'lam_re': 64.0,
     'b_glu': 25.292,
     'q_a_norm': 8.0,
     'kv_a_norm': 7.081,
     'out_norm_ssm': 45.964,
     'out_norm_attn': 45.764,
     'ffn_norm': 31.393,
     'conv_b': 45.484,
     'final_norm': 33.567,
     'b_re': 2.679,
     'c_re': 2.686,
     'c_im': 2.691}
    for name, (base, spread) in spreads.items():
        noise = np.random.default_rng([zlib.crc32(name.encode()), seed]).standard_normal(out[name].shape)
        drawn = base * np.exp(spread * noise) if base else spread * noise
        out[name] = __import__('jax').numpy.asarray(drawn.astype(out[name].dtype))
    for name, factor in factors.items():
        out[name] = (out[name] * factor).astype(out[name].dtype)
    return out


_narrow_inputs = first_inputs


def first_inputs(seed=0):

    out = dict(_narrow_inputs(seed))
    wider = {'lam_re': 12.0,
     'b_im': 3.11,
     'out_norm_ssm': 6.35,
     'out_norm_attn': 6.38,
     'ffn_norm': 4.37,
     'conv_b': 4.37,
     'final_norm': 6.52}
    for name, times in wider.items():
        mean = out[name].mean()
        out[name] = (mean + times * (out[name] - mean)).astype(out[name].dtype)
    return out


DEPTH_2 = 2

HEAD_DIM = 128
N_MIXERS = 4
HEADS_PER_MIXER = D_MODEL // HEAD_DIM // N_MIXERS
GROUP_WIDTH = HEADS_PER_MIXER * HEAD_DIM
MIX_WIDTH = N_MIXERS * GROUP_WIDTH
ROPE_THETA = 500000.0
ROPE_FRACTION = 4
NSA_KV_WIDTH = HEAD_DIM
NSA_CMP_BLOCK = 32
NSA_CMP_STRIDE = 16
NSA_CMP_HIDDEN = 256
NSA_SLC_BLOCK = 64
NSA_TOPK = 16
NSA_LOCAL_BLOCKS = 2
NSA_WINDOW = 512
DIFF_QK_DIM = HEAD_DIM // 2
D_FF_2 = 5632
CONV_WIDTH = 3
NEG_INF = -1e30
FORCE_SCORE = 1e9

IN_SPLITS = (
    GROUP_WIDTH,
    NSA_KV_WIDTH, NSA_KV_WIDTH,
    NSA_KV_WIDTH, NSA_KV_WIDTH,
    NSA_KV_WIDTH, NSA_KV_WIDTH,
    3 * HEADS_PER_MIXER,
    GROUP_WIDTH, GROUP_WIDTH, GROUP_WIDTH,
    GROUP_WIDTH, GROUP_WIDTH, GROUP_WIDTH, HEADS_PER_MIXER,
    GROUP_WIDTH, GROUP_WIDTH, GROUP_WIDTH,
)
IN_COLS = sum(IN_SPLITS)


def _rms_norm(x, g):
    xf = x.astype(jnp.float32)
    y = xf * lax.rsqrt(jnp.mean(xf * xf, axis=-1, keepdims=True) + EPS)
    return (y * g.astype(jnp.float32)).astype(x.dtype)

def _rope_tables(seq, rot_dim):
    pos = jnp.arange(seq, dtype=jnp.float32)
    inv = ROPE_THETA ** (-jnp.arange(0, rot_dim, 2, dtype=jnp.float32) / rot_dim)
    ang = pos[:, None] * inv[None, :]
    return jnp.cos(ang), jnp.sin(ang)

def _partial_rope(x, cos, sin):
    half = cos.shape[-1]
    rot = 2 * half
    xf = x.astype(jnp.float32)
    x1, x2, rest = xf[..., :half], xf[..., half:rot], xf[..., rot:]
    out = jnp.concatenate([x1 * cos - x2 * sin, x2 * cos + x1 * sin, rest], axis=-1)
    return out.astype(x.dtype)

def _heads(t, n_heads):
    b, s, _ = t.shape
    return t.reshape(b, s, n_heads, -1).transpose(0, 2, 1, 3)

def _merge_heads(o):
    b, h, s, d = o.shape
    return o.transpose(0, 2, 1, 3).reshape(b, s, h * d)

def _sweep(body, n_blocks):
    out = lax.map(body, jnp.arange(n_blocks))
    nb, b, h, qb, d = out.shape
    return out.transpose(1, 2, 0, 3, 4).reshape(b, h, nb * qb, d)

def _stick_breaking_attention(q, k, v):
    b, h, s_len, d = q.shape
    scale = d ** -0.5
    kpos = jnp.arange(s_len)

    def body(i):
        q0 = i * Q_BLOCK
        qb = lax.dynamic_slice_in_dim(q, q0, Q_BLOCK, axis=2)
        qpos = q0 + jnp.arange(Q_BLOCK)
        past = kpos[None, :] < qpos[:, None]
        z = jnp.einsum('bhqd,bhkd->bhqk', qb, k).astype(jnp.float32) * scale
        log_keep = jnp.where(past, jax.nn.log_sigmoid(-z), 0.0)
        after = lax.cumsum(log_keep, axis=3, reverse=True) - log_keep
        w = jnp.where(past, jnp.exp(jax.nn.log_sigmoid(z) + after), 0.0)
        return jnp.einsum('bhqk,bhkd->bhqd', w.astype(v.dtype), v)

    return _sweep(body, s_len // Q_BLOCK)

def _forgetting_attention(q, k, v, log_f):
    b, h, s_len, d = q.shape
    scale = d ** -0.5
    cum = jnp.cumsum(log_f, axis=-1)
    kpos = jnp.arange(s_len)

    def body(i):
        q0 = i * Q_BLOCK
        qb = lax.dynamic_slice_in_dim(q, q0, Q_BLOCK, axis=2)
        cq = lax.dynamic_slice_in_dim(cum, q0, Q_BLOCK, axis=2)
        qpos = q0 + jnp.arange(Q_BLOCK)
        causal = kpos[None, :] <= qpos[:, None]
        s = jnp.einsum('bhqd,bhkd->bhqk', qb, k).astype(jnp.float32) * scale
        s = s + cq[..., :, None] - cum[..., None, :]
        p = jax.nn.softmax(jnp.where(causal, s, NEG_INF), axis=-1)
        return jnp.einsum('bhqk,bhkd->bhqd', p.astype(v.dtype), v)

    return _sweep(body, s_len // Q_BLOCK)

def _differential_attention(q1, q2, k1, k2, v, lam):
    b, h, s_len, dq = q1.shape
    scale = dq ** -0.5
    kpos = jnp.arange(s_len)

    def body(i):
        q0 = i * Q_BLOCK
        qpos = q0 + jnp.arange(Q_BLOCK)
        causal = kpos[None, :] <= qpos[:, None]

        def probs(q, k):
            qb = lax.dynamic_slice_in_dim(q, q0, Q_BLOCK, axis=2)
            s = jnp.einsum('bhqd,bhkd->bhqk', qb, k).astype(jnp.float32) * scale
            return jax.nn.softmax(jnp.where(causal, s, NEG_INF), axis=-1)

        w = probs(q1, k1) - lam * probs(q2, k2)
        return jnp.einsum('bhqk,bhkd->bhqd', w.astype(v.dtype), v)

    return _sweep(body, s_len // Q_BLOCK)

def _nsa_attention(q, q_rot, k_cmp, v_cmp, k_slc, v_slc, k_win, v_win, gates,
                   pe_k, pe_v, cmp_k1, cmp_k2, cmp_v1, cmp_v2):
    b, h, s_len, d = q.shape
    scale = d ** -0.5
    n_c = (s_len - NSA_CMP_BLOCK) // NSA_CMP_STRIDE + 1
    n_sel = s_len // NSA_SLC_BLOCK
    tpos = jnp.arange(s_len)

    blk = np.arange(n_c)[:, None] * NSA_CMP_STRIDE + np.arange(NSA_CMP_BLOCK)[None, :]

    def compress(t, pe, w1, w2):
        tb = (t[:, blk] + pe).reshape(b, n_c, NSA_CMP_BLOCK * d)
        return jax.nn.gelu(tb @ w1) @ w2

    kc = compress(k_cmp, pe_k, cmp_k1, cmp_k2)
    vc = compress(v_cmp, pe_v, cmp_v1, cmp_v2)
    c_end = np.arange(n_c) * NSA_CMP_STRIDE + NSA_CMP_BLOCK - 1
    c_valid = c_end[None, :] <= tpos[:, None]
    sc = jnp.einsum('bhsd,bcd->bhsc', q, kc).astype(jnp.float32) * scale
    p_cmp = jax.nn.softmax(jnp.where(c_valid, sc, NEG_INF), axis=-1) * c_valid
    o_cmp = jnp.einsum('bhsc,bcd->bhsd', p_cmp.astype(vc.dtype), vc)

    overlap = np.zeros((n_c, n_sel), np.float32)
    for r in range(NSA_CMP_BLOCK // NSA_CMP_STRIDE):
        sub = np.arange(n_c) * NSA_CMP_STRIDE + r * NSA_CMP_STRIDE
        np.add.at(overlap, (np.arange(n_c), sub // NSA_SLC_BLOCK), 1.0)
    imp = jnp.einsum('bsc,cj->bsj', p_cmp.sum(axis=1), overlap)
    blk_id = jnp.arange(n_sel)
    cur = tpos // NSA_SLC_BLOCK
    sel_valid = blk_id[None, :] <= cur[:, None]
    forced = sel_valid & ((blk_id[None, :] == 0) |
                          (blk_id[None, :] >= cur[:, None] - (NSA_LOCAL_BLOCKS - 1)))
    score = jnp.where(forced, FORCE_SCORE, jnp.where(sel_valid, imp, NEG_INF))
    n_top = min(NSA_TOPK, n_sel)
    _, top_idx = lax.top_k(score, n_top)

    ks_blocks = k_slc.reshape(b, n_sel, NSA_SLC_BLOCK, d)
    vs_blocks = v_slc.reshape(b, n_sel, NSA_SLC_BLOCK, d)
    gather = jax.vmap(lambda blocks, idx: blocks[idx])

    def slc_body(i):
        q0 = i * Q_BLOCK
        qb = lax.dynamic_slice_in_dim(q_rot, q0, Q_BLOCK, axis=2)
        ib = lax.dynamic_slice_in_dim(top_idx, q0, Q_BLOCK, axis=1)
        ks = gather(ks_blocks, ib)
        vs = gather(vs_blocks, ib)
        qpos = q0 + jnp.arange(Q_BLOCK)
        kpos = ib[..., None] * NSA_SLC_BLOCK + jnp.arange(NSA_SLC_BLOCK)
        valid = kpos <= qpos[None, :, None, None]
        s = jnp.einsum('bhqd,bqnld->bhqnl', qb, ks).astype(jnp.float32) * scale
        s = jnp.where(valid[:, None], s, NEG_INF).reshape(b, h, Q_BLOCK, -1)
        p = jax.nn.softmax(s, axis=-1).reshape(b, h, Q_BLOCK, n_top, NSA_SLC_BLOCK)
        return jnp.einsum('bhqnl,bqnld->bhqd', p.astype(vs.dtype), vs)

    o_slc = _sweep(slc_body, s_len // Q_BLOCK)

    span = NSA_WINDOW + Q_BLOCK
    kw_pad = jnp.pad(k_win, ((0, 0), (NSA_WINDOW, 0), (0, 0)))
    vw_pad = jnp.pad(v_win, ((0, 0), (NSA_WINDOW, 0), (0, 0)))

    def win_body(i):
        q0 = i * Q_BLOCK
        qb = lax.dynamic_slice_in_dim(q_rot, q0, Q_BLOCK, axis=2)
        kb = lax.dynamic_slice_in_dim(kw_pad, q0, span, axis=1)
        vb = lax.dynamic_slice_in_dim(vw_pad, q0, span, axis=1)
        qpos = q0 + jnp.arange(Q_BLOCK)
        kpos = q0 - NSA_WINDOW + jnp.arange(span)
        valid = ((kpos[None, :] <= qpos[:, None]) & (kpos[None, :] > qpos[:, None] - NSA_WINDOW)
                 & (kpos[None, :] >= 0))
        s = jnp.einsum('bhqd,bkd->bhqk', qb, kb).astype(jnp.float32) * scale
        p = jax.nn.softmax(jnp.where(valid, s, NEG_INF), axis=-1)
        return jnp.einsum('bhqk,bkd->bhqd', p.astype(vb.dtype), vb)

    o_win = _sweep(win_body, s_len // Q_BLOCK)

    return gates[..., 0:1] * o_cmp + gates[..., 1:2] * o_slc + gates[..., 2:3] * o_win

def second_inputs(seed: int = 0) -> dict:
    key = jax.random.key(seed)
    ks = jax.random.split(key, 20)
    f32 = jnp.float32

    def nrm(k, shape, scale):
        return jax.random.normal(k, shape, f32) * scale

    def gain(k, shape):
        return 1.0 + 0.05 * jax.random.normal(k, shape, f32)

    cmp_in = NSA_CMP_BLOCK * HEAD_DIM
    return {
        'x': nrm(ks[0], (BATCH, SEQ, D_MODEL), 1.0),
        'norm_mix_pre': gain(ks[1], (DEPTH_2, D_MODEL)),
        'norm_mix_post': gain(ks[2], (DEPTH_2, D_MODEL)),
        'norm_mlp_pre': gain(ks[3], (DEPTH_2, D_MODEL)),
        'norm_mlp_post': gain(ks[4], (DEPTH_2, D_MODEL)),
        'w_in': nrm(ks[5], (DEPTH_2, D_MODEL, IN_COLS), D_MODEL ** -0.5),
        'w_out': nrm(ks[6], (DEPTH_2, MIX_WIDTH, D_MODEL), MIX_WIDTH ** -0.5),
        'nsa_pe_k': nrm(ks[7], (DEPTH_2, NSA_CMP_BLOCK, HEAD_DIM), 0.1),
        'nsa_pe_v': nrm(ks[8], (DEPTH_2, NSA_CMP_BLOCK, HEAD_DIM), 0.1),
        'nsa_cmp_k1': nrm(ks[9], (DEPTH_2, cmp_in, NSA_CMP_HIDDEN), cmp_in ** -0.5),
        'nsa_cmp_k2': nrm(ks[10], (DEPTH_2, NSA_CMP_HIDDEN, HEAD_DIM), NSA_CMP_HIDDEN ** -0.5),
        'nsa_cmp_v1': nrm(ks[11], (DEPTH_2, cmp_in, NSA_CMP_HIDDEN), cmp_in ** -0.5),
        'nsa_cmp_v2': nrm(ks[12], (DEPTH_2, NSA_CMP_HIDDEN, HEAD_DIM), NSA_CMP_HIDDEN ** -0.5),
        'fox_forget_bias': 2.0 + nrm(ks[13], (DEPTH_2, HEADS_PER_MIXER), 0.5),
        'diff_lambda': nrm(ks[14], (DEPTH_2, 4, DIFF_QK_DIM), 0.1),
        'diff_norm': gain(ks[15], (DEPTH_2, HEAD_DIM)),
        'mlp_w_up': nrm(ks[16], (DEPTH_2, D_MODEL, 2 * D_FF_2), D_MODEL ** -0.5),
        'mlp_conv_w': nrm(ks[17], (DEPTH_2, CONV_WIDTH, 2 * D_FF_2), 0.6),
        'mlp_conv_b': nrm(ks[18], (DEPTH_2, 2 * D_FF_2), 0.01),
        'mlp_w_down': nrm(ks[19], (DEPTH_2, D_FF_2, D_MODEL), D_FF_2 ** -0.5),
    }

def second_block(x, norm_mix_pre, norm_mix_post, norm_mlp_pre, norm_mlp_post, w_in, w_out,
              nsa_pe_k, nsa_pe_v, nsa_cmp_k1, nsa_cmp_k2, nsa_cmp_v1, nsa_cmp_v2,
              fox_forget_bias, diff_lambda, diff_norm, mlp_w_up, mlp_conv_w, mlp_conv_b,
              mlp_w_down):
    b, s_len, _ = x.shape
    h_n = HEADS_PER_MIXER
    cos_h, sin_h = _rope_tables(s_len, HEAD_DIM // ROPE_FRACTION)
    cos_d, sin_d = _rope_tables(s_len, DIFF_QK_DIM // ROPE_FRACTION)
    split_at = np.cumsum(IN_SPLITS)[:-1].tolist()

    for l in range(DEPTH_2):
        hin = _rms_norm(x, norm_mix_pre[l])
        proj = hin @ w_in[l]
        (a_q, a_kc, a_vc, a_ks, a_vs, a_kw, a_vw, a_g,
         b_q, b_k, b_v,
         c_q, c_k, c_v, c_f,
         d_q, d_k, d_v) = jnp.split(proj, split_at, axis=-1)

        qa = _heads(a_q, h_n)
        gates = jax.nn.sigmoid(a_g.reshape(b, s_len, h_n, 3).transpose(0, 2, 1, 3))
        o_a = _nsa_attention(qa, _partial_rope(qa, cos_h, sin_h), a_kc, a_vc,
                             _partial_rope(a_ks, cos_h, sin_h), a_vs,
                             _partial_rope(a_kw, cos_h, sin_h), a_vw, gates,
                             nsa_pe_k[l], nsa_pe_v[l], nsa_cmp_k1[l], nsa_cmp_k2[l],
                             nsa_cmp_v1[l], nsa_cmp_v2[l])

        o_b = _stick_breaking_attention(_heads(b_q, h_n), _heads(b_k, h_n), _heads(b_v, h_n))

        log_f = jax.nn.log_sigmoid((c_f + fox_forget_bias[l]).astype(jnp.float32)).transpose(0, 2, 1)
        o_c = _forgetting_attention(_heads(c_q, h_n), _heads(c_k, h_n), _heads(c_v, h_n), log_f)

        dqh = _heads(d_q, h_n)
        dkh = _heads(d_k, h_n)
        q1 = _partial_rope(dqh[..., :DIFF_QK_DIM], cos_d, sin_d)
        q2 = _partial_rope(dqh[..., DIFF_QK_DIM:], cos_d, sin_d)
        k1 = _partial_rope(dkh[..., :DIFF_QK_DIM], cos_d, sin_d)
        k2 = _partial_rope(dkh[..., DIFF_QK_DIM:], cos_d, sin_d)
        lam_init = 0.8 - 0.6 * math.exp(-0.3 * l)
        lp = diff_lambda[l].astype(jnp.float32)
        lam = jnp.exp(jnp.sum(lp[0] * lp[1])) - jnp.exp(jnp.sum(lp[2] * lp[3])) + lam_init
        o_d = _differential_attention(q1, q2, k1, k2, _heads(d_v, h_n), lam)
        o_d = _rms_norm(o_d, diff_norm[l]) * (1.0 - lam_init)

        mixed = jnp.concatenate([_merge_heads(o_a), _merge_heads(o_b),
                                 _merge_heads(o_c), _merge_heads(o_d)], axis=-1) @ w_out[l]
        x = x + _rms_norm(mixed, norm_mix_post[l])

        hin = _rms_norm(x, norm_mlp_pre[l])
        u = hin @ mlp_w_up[l]
        u_pad = jnp.pad(u, ((0, 0), (CONV_WIDTH - 1, 0), (0, 0)))
        conv = mlp_conv_b[l] + mlp_conv_w[l][0] * u_pad[:, 0:s_len]
        for tap in range(1, CONV_WIDTH):
            conv = conv + mlp_conv_w[l][tap] * u_pad[:, tap:tap + s_len]
        gate, up = jnp.split(conv, 2, axis=-1)
        y = (jax.nn.gelu(gate, approximate=True) * up) @ mlp_w_down[l]
        x = x + _rms_norm(y, norm_mlp_post[l])

    return x


def setup_inputs(seed=0):
    out = dict(first_inputs(seed))
    for name, value in second_inputs(seed + 1).items():
        if name != "x":
            out[name + "_2"] = value
    return out


def reference(
    x, meta_tokens, mix_norm, w_in, lam_re, lam_im, log_dt, b_re, b_im, c_re, c_im, d_skip,
    w_glu, b_glu, q_a_norm, w_q_b, kv_a_norm, w_kv_b, out_norm_ssm, out_norm_attn, w_out,
    ffn_norm, w_up, conv_w, conv_b, w_down, final_norm, norm_mix_pre_2, norm_mix_post_2,
    norm_mlp_pre_2, norm_mlp_post_2, w_in_2, w_out_2, nsa_pe_k_2, nsa_pe_v_2, nsa_cmp_k1_2,
    nsa_cmp_k2_2, nsa_cmp_v1_2, nsa_cmp_v2_2, fox_forget_bias_2, diff_lambda_2, diff_norm_2,
    mlp_w_up_2, mlp_conv_w_2, mlp_conv_b_2, mlp_w_down_2,
):
    x = first_block(
        x, meta_tokens, mix_norm, w_in, lam_re, lam_im, log_dt, b_re, b_im, c_re, c_im, d_skip,
        w_glu, b_glu, q_a_norm, w_q_b, kv_a_norm, w_kv_b, out_norm_ssm, out_norm_attn, w_out,
        ffn_norm, w_up, conv_w, conv_b, w_down, final_norm,
    )
    return second_block(
        x, norm_mix_pre_2, norm_mix_post_2, norm_mlp_pre_2, norm_mlp_post_2, w_in_2, w_out_2,
        nsa_pe_k_2, nsa_pe_v_2, nsa_cmp_k1_2, nsa_cmp_k2_2, nsa_cmp_v1_2, nsa_cmp_v2_2,
        fox_forget_bias_2, diff_lambda_2, diff_norm_2, mlp_w_up_2, mlp_conv_w_2, mlp_conv_b_2,
        mlp_w_down_2,
    )


_drawn_inputs = setup_inputs


def setup_inputs(seed=0):
    import zlib

    import numpy as np

    out = dict(_drawn_inputs(seed))
    spreads = {}
    factors = {'lam_re': 3.229,
     'norm_mix_pre_2': 8.0,
     'norm_mix_post_2': 8.0,
     'norm_mlp_pre_2': 8.0,
     'norm_mlp_post_2': 8.0,
     'nsa_pe_k_2': 8.0,
     'nsa_pe_v_2': 8.0,
     'nsa_cmp_k1_2': 8.0,
     'nsa_cmp_k2_2': 8.0,
     'nsa_cmp_v1_2': 8.0,
     'nsa_cmp_v2_2': 7.11,
     'fox_forget_bias_2': 8.0,
     'diff_lambda_2': 8.0,
     'diff_norm_2': 64.0,
     'mlp_conv_b_2': 28.234}
    for name, (base, spread) in spreads.items():
        noise = np.random.default_rng([zlib.crc32(name.encode()), seed]).standard_normal(out[name].shape)
        drawn = base * np.exp(spread * noise) if base else spread * noise
        out[name] = jnp.asarray(drawn.astype(out[name].dtype))
    for name, factor in factors.items():
        out[name] = (out[name] * factor).astype(out[name].dtype)
    return out
```

```python
import math
from contextlib import ExitStack

import concourse.bass as bass
import numpy as np
from concourse import mybir

F32 = mybir.dt.float32
F32R = mybir.dt.float32r
ALU = mybir.AluOpType
ACT = mybir.ActivationFunctionType

P = 128
D = 2048
DC = D // P
TILE = 2048
RAW = 4
EPS = 1e-6
NEG = -1e30

META, SEQ = 16, 256
T1 = META + SEQ
HEADS1 = 8
ROPE1 = 64
FF1 = 5504
PASSES1 = (15, 14, 14)
SCALE1 = 1.0 / math.sqrt(192)
QT1 = ((0, 80), (80, 128), (208, 64))
PAIRS = 32
STEPS = 9
KEYS1 = (80, 208, 272)

T2 = SEQ
FF2 = 5632
PASSES2 = (16, 14, 14)
LAYERS = 2
SCALE2 = 128 ** -0.5
SCALE_DIFF = 64 ** -0.5
NCMP = 15
CMPW = 16

TILES1 = dict(w_in=15, q_b=3, kv_b=2, glu=4, w_out=16)
N1 = sum(TILES1.values()) + 2 * sum(PASSES1) + DC * len(PASSES1)
TILES2 = dict(a=11, cmp=9, b=12, c=12, d=12, w_out=16)
N2 = sum(TILES2.values()) + 2 * sum(PASSES2) + DC * len(PASSES2)

V1 = {}
_at = 0
for _name, _n in (("mix", 16), ("ffn", 16), ("final", 16), ("ssm", 8), ("attn", 8), ("q_a", 4), ("kv_a", 2),
                  ("d_skip", 8), ("b_glu", 8), ("conv0", 43), ("conv1", 43), ("conv2", 43), ("conv_b", 43)):
    V1[_name] = _at
    _at += _n
NV1 = _at
V2 = {}
_at = 0
for _name, _n in (("mix_pre", 16), ("mix_post", 16), ("mlp_pre", 16), ("mlp_post", 16), ("diff_norm", 1),
                  ("pe_k", 32), ("pe_v", 32), ("conv0", 88), ("conv1", 88), ("conv2", 88), ("conv_b", 88),
                  ("forget", 4), ("lam", 4), ("lam_init", 1), ("one_less_init", 1)):
    V2[_name] = _at
    _at += _n
NV2 = _at

C1 = dict(ident=0, ones=128, rot=256, cos=384, sin=384 + T1, mask0=384 + 2 * T1, mask1=464 + 2 * T1,
          zero=672 + 2 * T1)
NC1 = 672 + 3 * T1
C2 = {}
_at = 0
for _name, _n in (("ident", 128), ("ones", 128), ("rot_h", 128), ("rot_d", 128), ("cos_h", 256), ("sin_h", 256),
                  ("cos_d", 256), ("sin_d", 256), ("causal", 256), ("tri_ge", 128), ("tri_le", 256),
                  ("past", 384), ("past_neg", 384), ("cmp", 32), ("cmp01", 2 * 16)):
    C2[_name] = _at
    _at += _n
NC2 = _at

TWO_PI = 2 * math.pi


def _low_bits_off(x, bits):
    m, e = math.frexp(x)
    return math.ldexp(math.floor(m * 2 ** bits) / 2 ** bits, e)


PI1 = _low_bits_off(TWO_PI, 11)
PI2 = _low_bits_off(TWO_PI - PI1, 11)
PI3 = TWO_PI - PI1 - PI2
MAGIC = 1.5 * 2 ** 23
PI_IN = 3.1415925


class Tile:

    def __init__(self, r, g, first):
        self.r, self.g = r, g
        self.n = r + 4 * g if not isinstance(g, int) or g else r
        self.i = r - first + 4 * g if not isinstance(g, int) or g else r - first

    def slot(self, ahead=0):
        return (self.r + ahead) % RAW

    def loaded(self, ahead=0):
        return 16 * ((self.r + ahead) // RAW + 1) + (16 * self.g if not isinstance(self.g, int) or self.g else 0)


def tiles(eng, first, last, body, head=0, tail=0):
    at = first
    for _ in range(min(head, last - first)):
        body(Tile(at, 0, first))
        at += 1
    turns = max(0, (last - tail - at) // 4)
    if turns > 1:
        with eng.Fori(0, turns) as g:
            for j in range(4):
                body(Tile(at + j, g, first))
        at += 4 * turns
    while at < last:
        body(Tile(at, 0, first))
        at += 1


class Builder:
    def __init__(self, nc, ctx):
        self.nc, self.ctx = nc, ctx
        self.base = 16512
        self.old_sems = []
        self.issued = 0
        self.serial = 0
        self.stopped = False

    def at(self, name, shape, offset, dtype=F32):
        self.serial += 1
        return self.nc.alloc_sbuf_tensor_at(f"{name}_{self.serial}", shape, dtype, offset=self.base + offset)


R_RAW = 0
R_WHI = R_RAW + RAW * TILE * 4
R_X = R_WHI + RAW * TILE * 4
CH = T1 * 4
R_XN = R_X + 16 * CH
R_F = R_XN + 32 * CH
R_Y = R_F + 32 * CH
R_C = R_Y + 16 * CH
R_C_SIZE = NC2 * 4 + 64
R_V = R_C + (R_C_SIZE + 31) // 32 * 32
R_S = R_V + (max(NV1, NV2) * 4 + 31) // 32 * 32
R_END = 212800


def build(nc, ins, outs, dbg=None, upto=None):
    ctx = ExitStack()
    with ctx:
        b = Builder(nc, ctx)
        assert R_S + 24000 < R_END, (R_S, R_END)
        sem = lambda n: ctx.enter_context(nc.semaphore(n))

        w_loaded = [sem(f"w_loaded{s}") for s in range(RAW)]
        w_hi = sem("w_hi")
        w_lo = sem("w_lo")
        w_used = sem("w_used")
        bank_free = sem("bank_free")
        stream_sems = [*w_loaded, w_hi, w_lo, w_used, bank_free]
        raw = b.at("raw", [P, RAW, TILE], R_RAW)
        whi = b.at("whi", [P, RAW, TILE], R_WHI, F32R)
        wlo = b.at("wlo", [P, RAW, TILE], R_RAW, F32R)
        eps = b.at("eps", [P, 1], R_END - 64)
        unused = b.at("unused", [P, 1], R_END - 32)
        G = [ctx.enter_context(nc.psum_tensor(f"gemm{s}", [P, 512], F32)) for s in range(RAW)]
        A = [ctx.enter_context(nc.psum_tensor(f"att{s}", [P, 512], F32)) for s in range(4)]
        stream = ins["stream"]

        class Phase:

            def __init__(self, name):
                self.name = name

            def __enter__(self):
                self.ctx = ExitStack()
                self.sems = []
                self.block = self.ctx.enter_context(nc.Block())
                return self

            def sem(self, name):
                s = nc.alloc_semaphore(f"{self.name}_{name}")
                self.sems.append(s)
                return s

            def __exit__(self, *a):
                self.ctx.__exit__(*a)
                if a[0] is not None:
                    return False
                for s in b.old_sems:
                    nc.release_semaphore(s)
                b.old_sems = self.sems
                return False

        def clear_old(sp):
            for s in b.old_sems:
                sp.sem_clear(s)

        def sp_loads(sp, limit, base, total):
            last = min(limit, total)
            if last <= b.issued:
                return

            def load(t):
                if t.r >= RAW:
                    sp.wait_ge(w_used, t.n - (RAW - 1))
                row = base + t.n
                sp.dma_start(raw[:, t.slot(), :], stream[bass.ds(row, 1) if not isinstance(row, int) else slice(row, row + 1)]
                             .rearrange("o p n -> (o p) n")).then_inc(w_loaded[t.slot()], 16)

            first = b.issued
            tiles(sp, first, last, load, head=max(0, RAW - first))
            b.issued = last

        def split_hi(act, t, ahead):
            act.wait_ge(w_loaded[t.slot(ahead)], t.loaded(ahead))
            if t.r + ahead >= RAW:
                act.wait_ge(w_used, t.n + (ahead - RAW + 1))
            act.copy(whi[:, t.slot(ahead), :], raw[:, t.slot(ahead), :]).then_inc(w_hi, 1)

        def split_lo(dve, t, ahead):
            dve.wait_ge(w_hi, t.n + (ahead + 1))
            dve.tensor_tensor(wlo[:, t.slot(ahead), :], raw[:, t.slot(ahead), :],
                              whi[:, t.slot(ahead), :].bitcast(F32), ALU.subtract).then_inc(w_lo, 1)

        def product(pe, out, left, right, nk, start=True, stop=True):
            for k in range(nk):
                (lh, ll), (rh, rl) = left(k), right(k)
                pe.matmul(out, lh, rh, start=(start and k == 0), stop=False)
                pe.matmul(out, lh, rl, start=False, stop=False)
                m = pe.matmul(out, ll, rh, start=False, stop=(stop and k == nk - 1))
            return m

        def weights(t, lo, n):
            return whi[:, t.slot(), lo:lo + n], wlo[:, t.slot(), lo:lo + n]

        def gemm(name, n0, n1, base, total, pe_tile, evac, act_tile=None, sems=(), flat=False, table=None, pe_end=None, act_end=None):
            with Phase(name) as ph:
                S = {k: ph.sem(k) for k in sems}
                tail = 4 if n1 + 2 > total else 0
                head = n1 - n0 if flat else max(0, RAW - n0)

                @ph.block.sync
                def _(sp):
                    clear_old(sp)
                    sp_loads(sp, n1 + RAW, base, total)

                @ph.block.scalar
                def _(act):
                    if n0 == 0:
                        for ahead in range(2):
                            split_hi(act, Tile(0, 0, 0), ahead)

                    def step(t):
                        if table and (t.r - n0) % 4 == 0:
                            act.activation(unused[:, :], eps[:, :], table)
                        if t.r + 2 < total:
                            split_hi(act, t, 2)
                        if act_tile:
                            act_tile(act, t, S)
                    tiles(act, n0, n1, step, head, tail)
                    if act_end:
                        act_end(act, S)

                @ph.block.vector
                def _(dve):
                    if n0 == 0:
                        for ahead in range(2):
                            split_lo(dve, Tile(0, 0, 0), ahead)

                    def step(t):
                        if t.r + 2 < total:
                            split_lo(dve, t, 2)
                        dve.wait_ge(w_used, t.n + 1)
                        m = evac(dve, t, S)
                        if m is None:
                            dve.sem_inc(bank_free, 1)
                        else:
                            m.then_inc(bank_free, 1)
                    tiles(dve, n0, n1, step, head, tail)

                @ph.block.tensor
                def _(pe):
                    def step(t):
                        pe.wait_ge(w_lo, t.n + 1)
                        if t.r >= RAW:
                            pe.wait_ge(bank_free, t.n - (RAW - 1))
                        pe_tile(pe, t, S).then_inc(w_used, 1)
                    tiles(pe, n0, n1, step, head, tail)
                    if pe_end:
                        pe_end(pe, S)

        def full_tile(xh, xl, T, nk=DC):
            def pe_tile(pe, t, S):
                return product(pe, G[t.slot()][:, 0:T], lambda k: weights(t, k * P, P),
                               lambda k: (xh[:, k, :], xl[:, k, :]), nk)
            return pe_tile

        def rms_norm(name, src, gains, chunks, T, dim, hi=None, lo=None, out=None, add=None, scratch=R_S, setup=None):
            with Phase(name) as ph:
                sq = b.at("sq", [P, 4, T], scratch)
                tmp = b.at("normed", [P, 4, T], scratch + 4 * CH)
                std = b.at("std", [P, T], scratch + 8 * CH)
                rstd = b.at("rstd", [P, T], scratch + 9 * CH)
                ready = ph.sem("ready")
                squared = ph.sem("squared")
                summed = ph.sem("summed")
                rooted = ph.sem("rooted")
                inverted = ph.sem("inverted")
                scaled = ph.sem("scaled")
                high = ph.sem("high")
                low = ph.sem("low")
                low_dve = ph.sem("low_dve")

                by_dve = lambda c: c % 4 == 1
                by_pool = lambda c: sum(1 for i in range(c + 1) if not by_dve(i))

                def finish(eng, c, dve_turn):
                    if by_dve(c) != bool(dve_turn):
                        return
                    if hi:
                        eng.wait_ge(high, c + 1)
                        m = eng.tensor_tensor(lo(c), tmp[:, c % 4, :], hi(c).bitcast(F32), ALU.subtract)
                    elif add:
                        eng.wait_ge(scaled, c + 1)
                        m = eng.tensor_tensor(add(c), add(c), tmp[:, c % 4, :], ALU.add)
                    else:
                        return
                    m.then_inc(low_dve if dve_turn else low, 1)

                @ph.block.sync
                def _(sp):
                    clear_old(sp)
                    if setup:
                        setup(sp, ready)

                @ph.block.scalar
                def _(act):
                    if setup:
                        act.wait_ge(ready, setup.count)
                    for c in range(chunks):
                        if c >= 4:
                            act.wait_ge(summed, c - 3)
                        act.activation(sq[:, c % 4, :], src(c), ACT.Square).then_inc(squared, 1)
                    act.wait_ge(summed, chunks)
                    act.activation(std[:, :], A[0][:, 0:T], ACT.Sqrt, bias=eps[:, 0:1], scale=1.0 / dim).then_inc(rooted, 1)
                    if hi:
                        for c in range(chunks):
                            act.wait_ge(scaled, c + 1)
                            act.activation(hi(c), tmp[:, c % 4, :], ACT.Copy).then_inc(high, 1)

                @ph.block.tensor
                def _(pe):
                    for c in range(chunks):
                        pe.wait_ge(squared, c + 1)
                        pe.matmul(A[0][:, 0:T], cst("ones", 128), sq[:, c % 4, :], start=(c == 0),
                                  stop=(c == chunks - 1)).then_inc(summed, 1)

                @ph.block.gpsimd
                def _(pool):
                    for c in range(chunks):
                        finish(pool, c, 0)

                @ph.block.vector
                def _(dve):
                    dve.wait_ge(rooted, 1)
                    dve.reciprocal(rstd[:, :], std[:, :]).then_inc(inverted, 1)
                    dve.wait_ge(inverted, 1)
                    if setup:
                        dve.wait_ge(ready, setup.count)
                    for c in range(chunks):
                        if (hi or add) and c >= 4:
                            if by_dve(c):
                                dve.wait_ge(low_dve, c // 4)
                            else:
                                dve.wait_ge(low, by_pool(c - 4))
                        dst = tmp[:, c % 4, :] if (hi or add) else out(c)
                        dve.scalar_tensor_tensor(out=dst, in0=src(c), scalar=gains(c), in1=rstd[:, :], op0=ALU.mult,
                                                 op1=ALU.mult).then_inc(scaled, 1)
                        if c >= 2:
                            finish(dve, c - 2, 1)
                    for c in range(max(0, chunks - 2), chunks):
                        finish(dve, c, 1)

        def attention(name, units, n_groups, take_out, at):
            with Phase(name) as ph:
                Sm = b.at("masked", [P, 2, T1], at)
                Pr = b.at("probs", [P, 3, T1], at + 2 * CH)
                PT = b.at("probs_t", [P, 2, 3 * 128], at + 5 * CH)
                dg = b.at("diag", [P, 2, 128], at + 5 * CH + 3072)
                st = b.at("stats", [P, 4, 4], at + 5 * CH + 3072 + 1024)
                scored = ph.sem("scored")
                masked = ph.sem("masked")
                maxed = ph.sem("maxed")
                expd = ph.sem("expd")
                inv = ph.sem("inv")
                diag = ph.sem("diag")
                turned = ph.sem("turned")
                copied = ph.sem("copied")
                valued = ph.sem("valued")
                taken_hi = ph.sem("taken_hi")
                taken = ph.sem("taken")
                U = len(units)
                ends = [max(i for i, u in enumerate(units) if u["group"] == g) for g in range(n_groups)]
                extra = 0
                inv_count = []
                for u in units:
                    extra += 2 if u["factor"] is not None else 1
                    inv_count.append(extra)

                @ph.block.sync
                def _(sp):
                    clear_old(sp)

                @ph.block.tensor
                def _(pe):
                    def scores(u):
                        x = units[u]
                        if u >= 2:
                            pe.wait_ge(masked, u - 1)
                        prs = x["scores"]
                        for j, (l, r, c0) in enumerate(prs):
                            m = pe.matmul(A[u % 2][0:x["nq"], c0:c0 + r.shape[-1]], l, r, start=(j == 0),
                                          stop=(j == len(prs) - 1), skip_group_check=True)
                        m.then_inc(scored, 1)

                    def turn(u):
                        x = units[u]
                        pe.wait_ge(diag, u + 1)
                        if u >= 2:
                            pe.wait_ge(copied, u - 1)
                        for j, (k0, kn) in enumerate(x["keys"]):
                            m = pe.matmul(A[2 + u % 2][0:kn, j * 128:j * 128 + x["nq"]], Pr[0:x["nq"], u % 3, k0:k0 + kn],
                                          dg[0:x["nq"], u % 2, 0:x["nq"]], start=True, stop=True)
                        m.then_inc(turned, 1)

                    def value(u):
                        x = units[u]
                        pe.wait_ge(copied, u + 1)
                        g = x["group"]
                        if x["first"] and g >= 2:
                            pe.wait_ge(taken, g - 1)
                        nkt = len(x["keys"])
                        for j, (k0, kn) in enumerate(x["keys"]):
                            m = pe.matmul(G[g % 2][:, 0:x["nq"]], x["values"][j], PT[0:kn, u % 2, j * 128:j * 128 + x["nq"]],
                                          start=(x["first"] and j == 0), stop=(x["last"] and j == nkt - 1))
                        m.then_inc(valued, 1)

                    for s in range(U + 3):
                        if s < U:
                            scores(s)
                        if 2 <= s < U + 2:
                            turn(s - 2)
                        if s >= 3:
                            value(s - 3)

                @ph.block.vector
                def _(dve):
                    def mask(u):
                        x = units[u]
                        nq, nk = x["nq"], x["nk"]
                        dve.wait_ge(scored, u + 1)
                        if u >= 2:
                            dve.wait_ge(expd, u - 1)
                        dve.tensor_tensor_reduce(Sm[0:nq, u % 2, 0:nk], A[u % 2][0:nq, 0:nk], x["mask"], 1.0, -3e38,
                                                 ALU.add, ALU.max, st[0:nq, 0, u % 4:u % 4 + 1]).then_inc(masked, 1)
                        dve.wait_ge(masked, u + 1)
                        dve.tensor_scalar(st[0:nq, 1, u % 4:u % 4 + 1], st[0:nq, 0, u % 4:u % 4 + 1], -1.0, None,
                                          ALU.mult).then_inc(maxed, 1)

                    def weigh(u):
                        x = units[u]
                        nq = x["nq"]
                        r = st[0:nq, 3, u % 4:u % 4 + 1]
                        dve.wait_ge(expd, u + 1)
                        dve.reciprocal(r, st[0:nq, 2, u % 4:u % 4 + 1]).then_inc(inv, 1)
                        if x["factor"] is not None:
                            dve.wait_ge(inv, inv_count[u] - 1)
                            dve.tensor_tensor(r, r, x["factor"], ALU.mult).then_inc(inv, 1)
                        dve.wait_ge(inv, inv_count[u])
                        if u >= 2:
                            dve.wait_ge(turned, u - 1)
                        keep = x.get("valid")
                        dve.tensor_scalar(dg[0:nq, u % 2, 0:nq], cst("ident", nq)[0:nq], r, keep, ALU.mult,
                                          *([ALU.mult] if keep is not None else [])).then_inc(diag, 1)

                    def out(u):
                        g = units[u]["group"]
                        if u == ends[g]:
                            take_out["dve"](dve, g, G[g % 2], units[u], taken_hi, valued, u + 1).then_inc(taken, 1)

                    for s in range(U + 4):
                        if s < U:
                            mask(s)
                        if 1 <= s < U + 1:
                            weigh(s - 1)
                        if s >= 4:
                            out(s - 4)

                @ph.block.scalar
                def _(act):
                    for s in range(U + 4):
                        if s < U:
                            x = units[s]
                            nq, nk = x["nq"], x["nk"]
                            act.wait_ge(maxed, s + 1)
                            if s >= 3:
                                act.wait_ge(turned, s - 2)
                            act.activation(Pr[0:nq, s % 3, 0:nk], Sm[0:nq, s % 2, 0:nk], ACT.Exp,
                                           bias=st[0:nq, 1, s % 4:s % 4 + 1],
                                           accum_out=st[0:nq, 2, s % 4:s % 4 + 1]).then_inc(expd, 1)
                        if 2 <= s < U + 2:
                            u = s - 2
                            x = units[u]
                            act.wait_ge(turned, u + 1)
                            if u >= 2:
                                act.wait_ge(valued, u - 1)
                            full = [j for j, (k0, kn) in enumerate(x["keys"]) if kn == 128]
                            rest = [(j, kn) for j, (k0, kn) in enumerate(x["keys"]) if kn != 128]
                            todo = []
                            if len(full) == 2 and x["nq"] == 128:
                                todo.append((128, 0, 256))
                            else:
                                todo += [(128, j * 128, x["nq"]) for j in full]
                            todo += [(kn, j * 128, x["nq"]) for j, kn in rest]
                            for q, (kn, c, w) in enumerate(todo):
                                m = act.activation(PT[0:kn, u % 2, c:c + w], A[2 + u % 2][0:kn, c:c + w], ACT.Copy)
                            m.then_inc(copied, 1)
                        if s >= 4:
                            u = s - 4
                            g = units[u]["group"]
                            if u == ends[g] and take_out.get("act"):
                                take_out["act"](act, g, G[g % 2], units[u], valued, u + 1).then_inc(taken_hi, 1)

        def rope(name, chunks, T, rot, cos, sin, at, dests=None):
            with Phase(name) as ph:
                t0 = b.at("rope_a", [P, 2, T], at)
                t1 = b.at("rope_b", [P, 2, T], at + 2 * CH)
                swapped = ph.sem("swapped")
                by_cos = ph.sem("by_cos")
                by_sin = ph.sem("by_sin")
                added = ph.sem("added")
                dests_ = dests or chunks

                @ph.block.sync
                def _(sp):
                    clear_old(sp)

                @ph.block.tensor
                def _(pe):
                    for c, x in enumerate(chunks):
                        if c >= 2:
                            pe.wait_ge(by_sin, c - 1)
                        pe.matmul(A[c % 2][:, 0:T], rot, x, start=True, stop=True).then_inc(swapped, 1)

                @ph.block.gpsimd
                def _(pool):
                    for c, x in enumerate(chunks):
                        if c >= 2:
                            pool.wait_ge(added, c - 1)
                        pool.tensor_tensor(t0[:, c % 2, :], x, cos, ALU.mult).then_inc(by_cos, 1)

                @ph.block.vector
                def _(dve):
                    for c, x in enumerate(chunks):
                        dve.wait_ge(swapped, c + 1)
                        if c >= 2:
                            dve.wait_ge(added, c - 1)
                        dve.tensor_tensor(t1[:, c % 2, :], A[c % 2][:, 0:T], sin, ALU.mult).then_inc(by_sin, 1)
                        dve.wait_ge(by_sin, c + 1)
                        dve.wait_ge(by_cos, c + 1)
                        dve.tensor_tensor(dests_[c], t0[:, c % 2, :], t1[:, c % 2, :], ALU.add).then_inc(added, 1)

        def dump(pairs):
            with Phase("dump") as ph:
                s = ph.sem("dump")

                @ph.block.sync
                def _(sp):
                    clear_old(sp)
                    for k, (dst, src) in enumerate(pairs):
                        sp.dma_start(dst, src).then_inc(s, 16)
                        sp.wait_ge(s, 16 * (k + 1))

        xT = b.at("xT", [P, DC, T1], R_X)
        xh = b.at("xh", [P, DC, T1], R_XN, F32R)
        xl = b.at("xl", [P, DC, T1], R_XN + 16 * CH, F32R)
        c1 = b.at("const1", [P, NC1], R_C)
        v1 = b.at("vec1", [P, NV1], R_V)
        cur = {"c": c1, "map": C1}

        def cst(name, n):
            return cur["c"][:, cur["map"][name]:cur["map"][name] + n]

        def g1(name):
            return lambda c: v1[:, V1[name] + c:V1[name] + c + 1]

        R_LAT = R_S + 3 * 4096
        R_ATT1 = R_LAT + CH
        base = 0
        total = N1

        def load1(sp, ready):
            for k, (dst, src) in enumerate(((xT[:, :, :], ins["hT"].rearrange("p (c t) -> p c t", c=DC)),
                                            (c1[:, :], ins["const1"]), (v1[:, :], ins["vec1"]))):
                sp.dma_start(dst, src).then_inc(ready, 16)
            sp_loads(sp, RAW, base, total)
        load1.count = 48

        with Phase("init") as ph:
            @ph.block.vector
            def _(dve):
                dve.memset(eps[:, :], EPS)

        rms_norm("norm_mix", lambda c: xT[:, c, :], g1("mix"), DC, T1, D, hi=lambda c: xh[:, c, :],
                 lo=lambda c: xl[:, c, :], setup=load1)
        if upto == "norm1":
            dump([(dbg[0], xh[:, :, :].bitcast(F32)), (dbg[1], xl[:, :, :].bitcast(F32))])
            return
        u1 = b.at("u", [P, 16, T1], R_Y)
        lat = b.at("latent", [P, 7, T1], R_LAT)
        n = 0

        def to_chunk(dst, T, scale=None):
            def evac(dve, t, S):
                return dve.tensor_scalar(dst(t.i), G[t.slot()][:, 0:T], 1.0 if scale is None else scale, None, ALU.mult)
            return evac

        def chunk_of(buf):
            return lambda i: buf[:, i, :] if isinstance(i, int) else buf[:, bass.ds(i, 1), :].rearrange("p o t -> p (o t)")

        gemm("w_in_u", n, n + 8, base, total, full_tile(xh, xl, T1), to_chunk(chunk_of(u1), T1))
        n += 8
        gemm("w_in_l", n, n + 7, base, total, full_tile(xh, xl, T1), to_chunk(chunk_of(lat), T1))
        n += 7
        if upto == "w_in":
            dump([(dbg[0], u1[:, 0:8, :]), (dbg[1], lat[:, :, :])])
            return
        qah = b.at("qa_hi", [P, 4, T1], R_XN, F32R)
        qal = b.at("qa_lo", [P, 4, T1], R_XN + 4 * CH, F32R)
        kvh = b.at("kv_hi", [P, 2, T1], R_XN + 8 * CH, F32R)
        kvl = b.at("kv_lo", [P, 2, T1], R_XN + 10 * CH, F32R)
        rms_norm("norm_qa", lambda c: lat[:, 1 + c, :], g1("q_a"), 4, T1, 512, hi=lambda c: qah[:, c, :],
                 lo=lambda c: qal[:, c, :])
        rms_norm("norm_kva", lambda c: lat[:, 5 + c, :], g1("kv_a"), 2, T1, 256, hi=lambda c: kvh[:, c, :],
                 lo=lambda c: kvl[:, c, :])
        qn = b.at("q_nope", [P, 8, T1], R_XN + 12 * CH)
        qp = b.at("q_pe", [P, 4, T1], R_XN + 20 * CH)
        kn = b.at("k_nope", [P, 8, T1], R_XN + 24 * CH)
        vv = b.at("values", [P, 3, 1024], R_S)
        if upto == "latent":
            dump([(dbg[0], qah[:, :, :].bitcast(F32)), (dbg[1], kvh[:, :, :].bitcast(F32))])
            return

        def lowrank(name, n0, count, nk, lat_hi, lat_lo, take, values=False):
            windows = (0, 128, T1 - 128)
            jobs = 6 if values else 16 // nk

            with Phase(name) as ph:
                made = ph.sem("made")
                taken = ph.sem("taken")

                @ph.block.sync
                def _(sp):
                    clear_old(sp)
                    sp_loads(sp, n0 + count + RAW, base, total)

                @ph.block.scalar
                def _(act):
                    for i in range(count):
                        split_hi(act, Tile(n0 + i, 0, n0), 2)

                @ph.block.vector
                def _(dve):
                    for i in range(count):
                        for c in range(jobs):
                            k = i * jobs + c
                            dve.wait_ge(made, k + 1)
                            take(dve, k, A[k % 4]).then_inc(taken, 1)
                        dve.sem_inc(bank_free, 1)
                        split_lo(dve, Tile(n0 + i, 0, n0), 2)

                @ph.block.tensor
                def _(pe):
                    for i in range(count):
                        t = Tile(n0 + i, 0, n0)
                        pe.wait_ge(w_lo, t.n + 1)
                        for c in range(jobs):
                            k = i * jobs + c
                            if k >= 4:
                                pe.wait_ge(taken, k - 3)
                            if values:
                                t0 = windows[c // 2]
                                m = product(pe, A[k % 4][:, :],
                                            lambda kc: (lat_hi[:, kc, t0:t0 + 128], lat_lo[:, kc, t0:t0 + 128]),
                                            lambda kc: weights(t, kc * 1024 + (c % 2) * 512, 512), nk)
                            else:
                                m = product(pe, A[k % 4][:, 0:T1], lambda kc: weights(t, (kc * jobs + c) * P, P),
                                            lambda kc: (lat_hi[:, kc, :], lat_lo[:, kc, :]), nk)
                            m.then_inc(made, 1)
                        pe.wait_ge(made, (i + 1) * jobs)
                        pe.sem_inc(w_used, 1)

        lowrank("w_q_b", n, 3, 4, qah, qal, lambda dve, k, bank: dve.tensor_scalar(
            qn[:, k, :] if k < 8 else qp[:, k - 8, :], bank[:, 0:T1], SCALE1, None, ALU.mult))
        n += 3
        lowrank("w_k_b", n, 1, 2, kvh, kvl, lambda dve, k, bank: dve.tensor_copy(kn[:, k, :], bank[:, 0:T1]))
        n += 1
        lowrank("w_v_b", n, 1, 2, kvh, kvl, lambda dve, k, bank: dve.tensor_copy(
            vv[:, k // 2, (k % 2) * 512:(k % 2) * 512 + 512], bank[:, :]), values=True)
        n += 1
        kpe = lat[:, 0, :]
        rope("rope1", [qp[:, c, :] for c in range(4)] + [kpe], T1, cst("rot", 128), cst("cos", T1), cst("sin", T1), R_ATT1)
        if upto == "qkv":
            dump([(dbg[0], qn[:, :, :]), (dbg[1], qp[:, :, :]), (dbg[2], kn[:, :, :]), (dbg[3], vv[:, :, :]), (dbg[4], kpe)])
            return

        key_tiles = (((0, 80, 0),), ((0, 128, 0), (128, 80, 1)), ((0, 128, 0), (128, 16, 1), (144, 128, 2)))
        units = []
        for h in range(HEADS1):
            half = slice(64 * (h % 2), 64 * (h % 2) + 64)
            for i, (q0, nq) in enumerate(QT1):
                nk = KEYS1[i]
                units.append(dict(
                    scores=[(qn[:, h, q0:q0 + nq], kn[:, h, 0:nk], 0), (qp[half, h // 2, q0:q0 + nq], kpe[half, 0:nk], 0)],
                    nq=nq, nk=nk, mask=cst(("mask0", "mask1", "zero")[i], nk)[0:nq],
                    keys=[(k0, kn_) for k0, kn_, _ in key_tiles[i]],
                    values=[vv[0:kn_, w, h * 128:(h + 1) * 128] for _, kn_, w in key_tiles[i]],
                    factor=None, group=len(units), first=True, last=True, h=h, q0=q0))

        def out1(dve, g, bank, u, taken_hi, valued, v):
            dve.wait_ge(valued, v)
            return dve.tensor_copy(u1[:, 8 + u["h"], u["q0"]:u["q0"] + u["nq"]], bank[:, 0:u["nq"]])

        attention("mla", units, len(units), dict(dve=out1), R_ATT1)
        if upto == "mla":
            dump([(dbg[0], u1[:, 8:16, :])])
            return

        s5raw = b.at("s5raw", [P, 96], R_XN + 32 * CH - 384)
        braw = b.at("b_raw", [P, 2, 1024], R_XN)
        bbar = b.at("b_bar", [P, 2, 1024], R_XN + 8192)
        bt_ = b.at("b_tmp", [P, 2, 1024], R_XN + 16384)
        sm = b.at("s5_small", [P, 16, 32], R_XN + 24576)
        ang = b.at("angle", [P, 2, STEPS * 32], R_XN + 26624)
        cnt = b.at("turns", [P, 2, STEPS * 32], R_XN + 26624 + 2304)
        BT = b.at("b_turned", [P, 2, 8, 128], R_S)
        Cw = b.at("c_weights", [P, 3, 1024], R_S + 8192)
        rot = b.at("rotations", [P, 2, STEPS, 32], R_S + 20480)
        mag = b.at("magnitude", [P, 32], R_S + 20480 + 2304)
        assert R_S + 20480 + 2304 + 128 < R_END - 64
        with Phase("s5_setup") as ph:
            landed = ph.sem("landed")
            step = ph.sem("step")
            dt_done = ph.sem("dt_done")
            decay = ph.sem("decay")
            mag_done = ph.sem("mag_done")
            sines = ph.sem("sines")
            bbar_done = ph.sem("bbar_done")
            turned = ph.sem("turned")
            angles = ph.sem("angles")
            bt_done = ph.sem("bt_done")
            neg = ph.sem("neg")
            lr_, li_, ld_ = (s5raw[:, 32 * k:32 * k + 32] for k in range(3))
            v = lambda k: sm[:, k, :]
            DT, AR, TH, LBR, LBI, DEN, T_A, T_B, FR, FI = (v(k) for k in range(10))

            @ph.block.sync
            def _(sp):
                clear_old(sp)
                sp.dma_start(s5raw[:, :], ins["s5"][:, 0:96]).then_inc(landed, 16)
                sp.dma_start(braw[:, :, :], ins["s5"][:, 96:96 + 2048].rearrange("p (a n) -> p a n", a=2)).then_inc(landed, 16)
                sp.dma_start(Cw[:, 0, :], ins["s5"][:, 2144:2144 + 1024]).then_inc(landed, 16)
                sp.dma_start(Cw[:, 2, :], ins["s5"][:, 3168:3168 + 1024]).then_inc(landed, 16)

            @ph.block.gpsimd
            def _(pool):
                pool.wait_ge(landed, 64)
                pool.tensor_scalar(Cw[:, 1, :], Cw[:, 0, :], -1.0, None, ALU.mult).then_inc(neg, 1)
                pool.tensor_scalar(Cw[:, 2, :], Cw[:, 2, :], -1.0, None, ALU.mult).then_inc(neg, 1)

            @ph.block.scalar
            def _(act):
                act.wait_ge(landed, 64)
                act.activation(DT, ld_, ACT.Exp).then_inc(dt_done, 1)
                act.wait_ge(decay, 1)
                act.activation(mag[:, :], AR, ACT.Exp).then_inc(mag_done, 1)
                act.wait_ge(angles, 1)
                act.activation(rot[:, :, :, :].rearrange("p a j q -> p (a j q)"), ang[:, :, :].rearrange("p a n -> p (a n)"),
                               ACT.Sin).then_inc(sines, 1)
                for k in range(4):
                    act.wait_ge(turned, 4 * k + 4)
                    act.activation(BT[:, k // 2, 4 * (k % 2):4 * (k % 2) + 4, :].rearrange("p c n -> p (c n)"), A[k][:, :],
                                   ACT.Copy).then_inc(bt_done, 1)

            @ph.block.tensor
            def _(pe):
                pe.wait_ge(bbar_done, 2)
                for part in range(2):
                    for c in range(8):
                        k = part * 8 + c
                        pe.transpose(A[k // 4][:, (k % 4) * 128:(k % 4) * 128 + 128], bbar[:, part, c * 128:(c + 1) * 128],
                                     cst("ident", 128)).then_inc(turned, 1)

            @ph.block.vector
            def _(dve):
                count = [0]

                def link(ins_):
                    count[0] += 1
                    ins_.then_inc(step, 1)
                    dve.wait_ge(step, count[0])

                dve.wait_ge(dt_done, 1)
                dve.tensor_tensor(AR, lr_, DT, ALU.mult).then_inc(decay, 1)
                link(dve.tensor_tensor(TH, li_, DT, ALU.mult))
                for a in range(2):
                    for j in range(STEPS):
                        last = dve.tensor_scalar(ang[:, a, 32 * j:32 * j + 32], TH, float(2 ** j), None, ALU.mult)
                link(last)
                link(dve.tensor_scalar(cnt[:, 0, :], ang[:, 0, :], 1 / TWO_PI, 0.25, ALU.mult, ALU.add))
                link(dve.tensor_scalar(cnt[:, 1, :], ang[:, 1, :], 1 / TWO_PI, None, ALU.mult))
                link(dve.tensor_scalar(cnt[:, :, :], cnt[:, :, :], MAGIC, None, ALU.add))
                link(dve.tensor_scalar(cnt[:, :, :], cnt[:, :, :], -MAGIC, None, ALU.add))
                for part in (PI1, PI2, PI3):
                    link(dve.scalar_tensor_tensor(out=ang[:, :, :], in0=cnt[:, :, :], scalar=-part, in1=ang[:, :, :],
                                                  op0=ALU.mult, op1=ALU.add))
                link(dve.tensor_scalar(ang[:, 0, :], ang[:, 0, :], math.pi / 2, None, ALU.add))
                dve.tensor_scalar(ang[:, :, :], ang[:, :, :], PI_IN, -PI_IN, ALU.min, ALU.max).then_inc(angles, 1)
                dve.wait_ge(sines, 1)
                dve.wait_ge(mag_done, 1)
                dve.tensor_tensor(LBR, mag[:, :], rot[:, 0, 0, :], ALU.mult)
                dve.tensor_tensor(LBI, mag[:, :], rot[:, 1, 0, :], ALU.mult)
                dve.tensor_tensor(DEN, lr_, lr_, ALU.mult)
                link(dve.tensor_tensor(T_A, li_, li_, ALU.mult))
                dve.tensor_scalar(LBR, LBR, -1.0, None, ALU.add)
                link(dve.tensor_tensor(DEN, DEN, T_A, ALU.add))
                link(dve.reciprocal(DEN, DEN))
                dve.tensor_tensor(FR, LBR, lr_, ALU.mult)
                link(dve.tensor_tensor(T_A, LBI, li_, ALU.mult))
                dve.tensor_tensor(FI, LBI, lr_, ALU.mult)
                link(dve.tensor_tensor(T_B, LBR, li_, ALU.mult))
                dve.tensor_tensor(FR, FR, T_A, ALU.add)
                link(dve.tensor_tensor(FI, FI, T_B, ALU.subtract))
                dve.tensor_tensor(FR, FR, DEN, ALU.mult)
                link(dve.tensor_tensor(FI, FI, DEN, ALU.mult))
                wide = lambda f: f.unsqueeze(2).to_broadcast([P, 32, 32])
                m3 = lambda x: x.rearrange("p (q c) -> p q c", q=32)
                dve.tensor_tensor(m3(bbar[:, 0, :]), m3(braw[:, 0, :]), wide(FR), ALU.mult)
                dve.tensor_tensor(m3(bbar[:, 1, :]), m3(braw[:, 1, :]), wide(FR), ALU.mult)
                dve.tensor_tensor(m3(bt_[:, 0, :]), m3(braw[:, 1, :]), wide(FI), ALU.mult)
                link(dve.tensor_tensor(m3(bt_[:, 1, :]), m3(braw[:, 0, :]), wide(FI), ALU.mult))
                dve.tensor_tensor(bbar[:, 0, :], bbar[:, 0, :], bt_[:, 0, :], ALU.subtract).then_inc(bbar_done, 1)
                dve.tensor_tensor(bbar[:, 1, :], bbar[:, 1, :], bt_[:, 1, :], ALU.add).then_inc(bbar_done, 1)

        tab = b.at("rotation_table", [P, 2, 16, T1], R_F)
        tmp_c = b.at("table_tmp_c", [P, 16, 144], R_XN)
        tmp_s = b.at("table_tmp_s", [P, 16, 144], R_XN + 9216)
        rotated = b.at("rotated", [P, 2, 2, T1], R_XN)
        part_ = b.at("rotate_tmp", [P, 2, 4, T1], R_XN + 4 * CH)
        scanned = b.at("scanned", [P, 2, 2, T1], R_XN + 12 * CH)
        prod = b.at("products", [P, 2, 4, T1], R_XN + 16 * CH)

        def s5_table(half):
            with Phase(f"s5_table{half}") as ph:
                cos_to = ph.sem("cos_to")
                sin_to = ph.sem("sin_to")
                cos_part = ph.sem("cos_part")
                sin_part = ph.sem("sin_part")
                spans = [(2 ** j, min(2 ** j, T1 - 2 ** j)) for j in range(STEPS)]
                turn = lambda a, j, w: rot[:, a, j, 16 * half:16 * half + 16].unsqueeze(2).to_broadcast([P, 16, w])

                @ph.block.sync
                def _(sp):
                    clear_old(sp)

                def build_part(eng, mine, own, theirs, own_part, tmp, first_of, second_of, op):
                    eng.memset(tab[:, mine, :, 0:1], 1.0 - mine).then_inc(own, 1)
                    for j, (k, w) in enumerate(spans):
                        eng.wait_ge(theirs, j + 1)
                        eng.wait_ge(own, j + 1)
                        eng.tensor_tensor(tab[:, mine, :, k:k + w], tab[:, 0, :, 0:w], turn(first_of, j, w), ALU.mult).then_inc(own_part, 1)
                        eng.tensor_tensor(tmp[:, :, 0:w], tab[:, 1, :, 0:w], turn(second_of, j, w), ALU.mult).then_inc(own_part, 1)
                        eng.wait_ge(own_part, 2 * j + 2)
                        eng.tensor_tensor(tab[:, mine, :, k:k + w], tab[:, mine, :, k:k + w], tmp[:, :, 0:w], op).then_inc(own, 1)

                @ph.block.vector
                def _(dve):
                    build_part(dve, 0, cos_to, sin_to, cos_part, tmp_c, 0, 1, ALU.subtract)

                @ph.block.gpsimd
                def _(pool):
                    build_part(pool, 1, sin_to, cos_to, sin_part, tmp_s, 1, 0, ALU.add)

        def s5_main(half):
            with Phase(f"s5_main{half}") as ph:
                fed = ph.sem("fed")
                parts = ph.sem("parts")
                turned = ph.sem("turned")
                scan = ph.sem("scan")
                back = ph.sem("back")
                read = ph.sem("read")
                taken = ph.sem("taken")
                N = 16
                banks = [*A, G[2], G[3]]
                cs = lambda q: tab[:, 0, q, :]
                sn = lambda q: tab[:, 1, q, :]

                @ph.block.sync
                def _(sp):
                    clear_old(sp)

                @ph.block.tensor
                def _(pe):
                    def feed(q):
                        c, j = divmod(16 * half + q, 4)
                        if q >= 3:
                            pe.wait_ge(parts, q - 2)
                        for part in range(2):
                            m = pe.matmul(banks[2 * (q % 3) + part][:, 0:T1], BT[32 * j:32 * j + 32, part, c, :],
                                          u1[32 * j:32 * j + 32, c, :], start=True, stop=True)
                        m.then_inc(fed, 1)

                    def readout(q):
                        gq = 16 * half + q
                        c, j = divmod(gq, 4)
                        if j == 0 and q >= 8:
                            pe.wait_ge(taken, q // 4 - 1)
                        pe.wait_ge(back, q + 1)
                        for k, w in enumerate((0, 1, 2, 2)):
                            m = pe.matmul(G[c % 2][32 * j:32 * j + 32, 0:T1], Cw[:, w, 32 * gq:32 * gq + 32],
                                          prod[:, q % 2, k, :], start=(k == 0), stop=(k == 3))
                        m.then_inc(read, 1)

                    for q in range(3):
                        feed(q)
                    for q in range(N):
                        if q + 3 < N:
                            feed(q + 3)
                        readout(q)

                @ph.block.gpsimd
                def _(pool):
                    for q in range(N):
                        pool.wait_ge(scan, 2 * q + 2)
                        if q >= 2:
                            pool.wait_ge(read, q - 1)
                        gr, gi = scanned[:, q % 2, 0, :], scanned[:, q % 2, 1, :]
                        for k, (x, y) in enumerate(((gr, cs(q)), (gi, sn(q)), (gr, sn(q)), (gi, cs(q)))):
                            m = pool.tensor_tensor(prod[:, q % 2, k, :], x, y, ALU.mult)
                        m.then_inc(back, 1)

                @ph.block.vector
                def _(dve):
                    def multiply(q):
                        dve.wait_ge(fed, q + 1)
                        if q >= 2:
                            dve.wait_ge(turned, q - 1)
                        br, bi = (banks[2 * (q % 3) + part][:, 0:T1] for part in range(2))
                        for k, (x, y) in enumerate(((br, cs(q)), (bi, sn(q)), (bi, cs(q)), (br, sn(q)))):
                            m = dve.tensor_tensor(part_[:, q % 2, k, :], x, y, ALU.mult)
                        m.then_inc(parts, 1)

                    def rotate(q):
                        dve.wait_ge(parts, q + 1)
                        if q >= 2:
                            dve.wait_ge(scan, 2 * q - 2)
                        dve.tensor_tensor(rotated[:, q % 2, 0, :], part_[:, q % 2, 0, :], part_[:, q % 2, 1, :], ALU.add)
                        dve.tensor_tensor(rotated[:, q % 2, 1, :], part_[:, q % 2, 2, :], part_[:, q % 2, 3, :],
                                          ALU.subtract).then_inc(turned, 1)

                    def scan_(q):
                        dve.wait_ge(turned, q + 1)
                        if q >= 2:
                            dve.wait_ge(back, q - 1)
                        r = mag[:, 16 * half + q:16 * half + q + 1].to_broadcast([P, T1])
                        for part in range(2):
                            dve.tensor_tensor_scan(scanned[:, q % 2, part, :], r, rotated[:, q % 2, part, :], 0.0,
                                                   ALU.mult, ALU.add).then_inc(scan, 1)

                    def take(q):
                        c = (16 * half + q) // 4
                        dve.wait_ge(read, q + 1)
                        dve.scalar_tensor_tensor(out=u1[:, c, :], in0=u1[:, c, :], scalar=g1("d_skip")(c),
                                                 in1=G[c % 2][:, 0:T1], op0=ALU.mult, op1=ALU.add).then_inc(taken, 1)

                    multiply(0)
                    rotate(0)
                    for q in range(N):
                        if q + 1 < N:
                            multiply(q + 1)
                        scan_(q)
                        if q + 1 < N:
                            rotate(q + 1)
                        if q >= 2 and (q - 2) % 4 == 3:
                            take(q - 2)
                    take(N - 1)

        for half in range(2):
            s5_table(half)
            s5_main(half)
        if upto == "s5":
            dump([(dbg[0], u1[:, 0:8, :])])
            return

        gh = b.at("g_hi", [P, 8, T1], R_XN, F32R)
        gl = b.at("g_lo", [P, 8, T1], R_XN + 8 * CH, F32R)
        with Phase("gelu1") as ph:
            made = ph.sem("made")
            high = ph.sem("high")

            @ph.block.sync
            def _(sp):
                clear_old(sp)

            @ph.block.scalar
            def _(act):
                for c in range(8):
                    act.activation(u1[:, c, :], u1[:, c, :], ACT.Gelu_apprx_tanh).then_inc(made, 1)
                for c in range(8):
                    act.wait_ge(made, c + 1)
                    act.activation(gh[:, c, :], u1[:, c, :], ACT.Copy).then_inc(high, 1)

            @ph.block.vector
            def _(dve):
                for c in range(8):
                    dve.wait_ge(high, c + 1)
                    dve.tensor_tensor(gl[:, c, :], u1[:, c, :], gh[:, c, :].bitcast(F32), ALU.subtract)

        gate = b.at("gate", [P, 2, 2, T1], R_S)

        def glu_tile(pe, t, S):
            for e in range(2):
                bank = (G, A)[e][t.slot()]
                m = product(pe, bank[:, 0:T1], lambda k: weights(t, k * 256 + e * P, P),
                            lambda k: (gh[:, k, :], gl[:, k, :]), 8)
            return m

        def glu_act(act, t, S):
            act.wait_ge(w_used, t.n + 1)
            if t.i >= 2:
                act.wait_ge(bank_free, t.n - 1)
            for e in range(2):
                c = 2 * t.i + e
                m = act.activation(gate[:, t.i % 2, e, :], (G, A)[e][t.slot()][:, 0:T1], ACT.Sigmoid,
                                   bias=g1("b_glu")(c))
            m.then_inc(S["gated"], 1)

        def glu_evac(dve, t, S):
            dve.wait_ge(S["gated"], t.i + 1)
            for e in range(2):
                c = 2 * t.i + e
                m = dve.tensor_tensor(u1[:, c, :], u1[:, c, :], gate[:, t.i % 2, e, :], ALU.mult)
            return m

        gemm("w_glu", n, n + 4, base, total, glu_tile, glu_evac, glu_act, sems=("gated",))
        n += 4
        fh1 = b.at("f_hi", [P, 16, T1], R_F, F32R)
        fl1 = b.at("f_lo", [P, 16, T1], R_F + 16 * CH, F32R)
        for k, gname in enumerate(("ssm", "attn")):
            rms_norm(f"norm_{gname}", lambda c: u1[:, 8 * k + c, :], g1(gname), 8, T1, 1024,
                     hi=lambda c: fh1[:, 8 * k + c, :], lo=lambda c: fl1[:, 8 * k + c, :])
        if upto == "mix":
            dump([(dbg[0], fh1[:, :, :].bitcast(F32))])
            return

        def add_chunk(buf_of, T):
            def evac(dve, t, S):
                return dve.tensor_tensor(buf_of(t.i), buf_of(t.i), G[t.slot()][:, 0:T], ALU.add)
            return evac

        x_of = chunk_of(xT)
        gemm("w_out1", n, n + 16, base, total, full_tile(fh1, fl1, T1), add_chunk(x_of, T1))
        n += 16
        rms_norm("norm_ffn1", x_of, g1("ffn"), DC, T1, D, hi=lambda c: xh[:, c, :], lo=lambda c: xl[:, c, :])

        def feed_forward(name, n, passes, T, xh, xl, fh, fl, vec, vmap, both, silu, down_evac, base, total):
            cv = b.at("conv", [P, 2, T], R_S)
            cg = b.at("conv_gate", [P, 2, T], R_S + 2 * CH)
            ac = b.at("acted", [P, 2, T], R_S + 4 * CH)
            hid = b.at("hidden", [P, 2, T], R_S + 6 * CH)
            F = sum(passes)
            off = 0
            for p, np_ in enumerate(passes):
                col = lambda key, k: (vec[:, vmap[key] + k:vmap[key] + k + 1] if isinstance(k, int)
                                      else vec[:, bass.ds(k + vmap[key], 1)])
                steps = 4 if both else 2

                def convolve(dve, t, dst, k, S, done):
                    u = G[t.slot()]
                    dve.tensor_scalar(dst, u[:, 0:T], col("conv2", k), col("conv_b", k), ALU.mult, ALU.add).then_inc(S["conv"], 1)
                    dve.wait_ge(S["conv"], done + 1)
                    dve.scalar_tensor_tensor(out=dst[:, 1:T], in0=u[:, 0:T - 1], scalar=col("conv1", k), in1=dst[:, 1:T],
                                             op0=ALU.mult, op1=ALU.add).then_inc(S["conv"], 1)
                    dve.wait_ge(S["conv"], done + 2)
                    return dve.scalar_tensor_tensor(out=dst[:, 2:T], in0=u[:, 0:T - 2], scalar=col("conv0", k),
                                                    in1=dst[:, 2:T], op0=ALU.mult, op1=ALU.add)

                def evac(dve, t, S, off=off):
                    odd = (t.r - n) % 2
                    jr = (t.r - n) // 2
                    j = jr + 2 * t.g if not isinstance(t.g, int) or t.g else jr
                    if not odd:
                        return convolve(dve, t, cg[:, jr % 2, :], j + off, S, j * steps)
                    if both:
                        convolve(dve, t, cv[:, jr % 2, :], j + (off + F), S, j * 4 + 2).then_inc(S["value"], 1)
                        dve.wait_ge(S["value"], j + 1)
                        val = cv[:, jr % 2, :]
                    else:
                        val = G[t.slot()][:, 0:T]
                    dve.wait_ge(S["acted"], j + 1)
                    dve.tensor_tensor(hid[:, jr % 2, :], ac[:, jr % 2, :], val, ALU.mult).then_inc(S["hid"], 1)
                    dve.wait_ge(S["hid"], j + 1)
                    f_hi, f_lo = chunk_of(fh)(j), chunk_of(fl)(j)
                    dve.tensor_scalar(f_hi, hid[:, jr % 2, :], 1.0, None, ALU.mult).then_inc(S["fhi"], 1)
                    dve.wait_ge(S["fhi"], j + 1)
                    return dve.tensor_tensor(f_lo, hid[:, jr % 2, :], f_hi.bitcast(F32), ALU.subtract)

                def act_tile(act, t, S):
                    if (t.r - n) % 2 == 0:
                        return
                    jr = (t.r - n) // 2
                    act.wait_ge(bank_free, t.n)
                    act.activation(ac[:, jr % 2, :], cg[:, jr % 2, :], ACT.Silu if silu else ACT.Gelu_apprx_tanh).then_inc(S["acted"], 1)

                gemm(f"{name}_up{p}", n, n + 2 * np_, base, total, full_tile(xh, xl, T), evac, act_tile,
                     sems=("conv", "acted", "hid", "fhi", "value"), table=ACT.Silu if silu else ACT.Gelu_apprx_tanh)
                n += 2 * np_
                gemm(f"{name}_down{p}", n, n + DC, base, total, full_tile(fh, fl, T, np_), down_evac(p))
                n += DC
                off += np_
            return n

        n = feed_forward("ffn1", n, PASSES1, T1, xh, xl, fh1, fl1, v1, V1, False, True, lambda p: add_chunk(x_of, T1), base, total)
        assert n == N1, (n, N1)
        if upto == "ffn1":
            dump([(dbg[0], xT[:, :, :])])
            return
        rms_norm("norm_final", x_of, g1("final"), DC, T1, D, out=x_of)
        if upto == "block1":
            dump([(dbg[0], xT[:, :, :])])
            return

        c2 = b.at("const2", [P, NC2], R_C)
        v2 = b.at("vec2", [P, NV2], R_V)
        cur.update(c=c2, map=C2)
        X = lambda i: (xT[:, i, META:T1] if isinstance(i, int)
                       else xT[:, bass.ds(i, 1), META:T1].rearrange("p o t -> p (o t)"))
        xh2 = b.at("xh2", [P, DC, T2], R_XN, F32R)
        xl2 = b.at("xl2", [P, DC, T2], R_XN + DC * T2 * 4, F32R)
        fh2 = b.at("f_hi2", [P, DC, T2], R_F, F32R)
        fl2 = b.at("f_lo2", [P, DC, T2], R_F + DC * T2 * 4, F32R)
        y2 = b.at("y2", [P, DC, T2], R_Y)
        K4 = 4096
        q4 = b.at("q4", [P, 4, T2], R_Y)
        k4 = b.at("k4", [P, 4, T2], R_Y + K4)
        v4 = b.at("v4", [P, 2, 512], R_Y + 2 * K4)
        qr = b.at("q_turned", [P, 4, T2], R_Y + 3 * K4)
        kvc = b.at("kv_compress", [P, 2, T1], R_Y + 2 * K4)
        kvs = b.at("kv_rest", [P, 4, T2], R_Y + K4)
        R_FREE = R_S + 10240
        small = b.at("small", [P, 2, 16], R_FREE)
        gates = b.at("gates", [P, 2, 12], R_FREE + 128)
        flog = b.at("log_forget", [P, 4, 8], R_FREE + 256)
        lamb = b.at("lambda", [P, 16], R_FREE + 384)
        kcmp = b.at("k_cmp", [P, CMPW], R_FREE + 512)
        vcmp = b.at("v_cmp", [CMPW, 128], R_FREE + 640)
        tb = b.at("blocks", [P, 512], R_FREE + 1280)
        hidg = b.at("cmp_hidden", [CMPW, 2, 256], R_FREE + 1280)
        BW = 512 + 7 * CMPW
        tbh = b.at("blocks_hi", [P, 2, BW], R_FREE + 1280 + 2048, F32R)
        tbl = b.at("blocks_lo", [P, 2, BW], R_FREE + 1280 + 2048 + 5120, F32R)
        hidh = b.at("cmp_hidden_hi", [P, 4, 128], R_FREE + 1280 + 2048 + 10240, F32R)
        hidl = b.at("cmp_hidden_lo", [P, 4, 128], R_FREE + 1280 + 2048 + 10240 + 2048, F32R)
        assert R_FREE + 1280 + 2048 + 10240 + 4096 <= R_END - 64
        upright = b.at("upright", [P, 2, T2], R_S)

        def g2(name):
            return lambda c: v2[:, V2[name] + c:V2[name] + c + 1]

        def flush(sems):
            with nc.Block() as blk:
                @blk.sync
                def _(sp):
                    for s in [*b.old_sems, *sems]:
                        sp.sem_clear(s)
            for s in b.old_sems:
                nc.release_semaphore(s)
            b.old_sems = []

        def layer(l, base, stop=None):
            total = N2
            b.issued = 0

            def load2(sp, ready):
                row = bass.ds(l, 1) if not isinstance(l, int) else slice(l, l + 1)
                sp.dma_start(v2[:, :], ins["vec2"][row].rearrange("o p n -> (o p) n")).then_inc(ready, 16)
                sp.dma_start(c2[:, :], ins["const2"]).then_inc(ready, 16)
                sp_loads(sp, RAW, base, total)
            load2.count = 32
            rms_norm("mix_pre", X, g2("mix_pre"), DC, T2, D, hi=lambda c: xh2[:, c, :], lo=lambda c: xl2[:, c, :],
                     setup=load2)
            n = 0

            def turning(first, jobs):
                def lay_down(dve, t, S):
                    k = t.i - first
                    if k >= 2:
                        dve.wait_ge(S["turned"], k - 1)
                    return dve.tensor_copy(upright[:, k % 2, :], G[t.slot()][:, 0:T2])

                def turn(pe, k, n_of, S):
                    rows = jobs[k][1]
                    pe.wait_ge(bank_free, n_of + 1)
                    if k >= 2:
                        pe.wait_ge(S["copied"], k - 1)
                    for i in range(2):
                        m = pe.transpose(A[k % 2][:, i * rows:(i + 1) * rows], upright[0:rows, k % 2, i * P:(i + 1) * P],
                                         cst("ident", rows)[0:rows])
                    m.then_inc(S["turned"], 1)

                def copy_out(act, k, S):
                    dst, rows = jobs[k]
                    act.wait_ge(S["turned"], k + 1)
                    act.copy(dst, A[k % 2][:, 0:2 * rows].rearrange("p (a d) -> p a d", a=2)).then_inc(S["copied"], 1)
                return lay_down, turn, copy_out

            full = full_tile(xh2, xl2, T2)

            as2 = lambda x: x.rearrange("p (a d) -> p a d", a=2)
            lay_s, turn_s, copy_s = turning(8, [(as2(kvs[:, 2, :]), P), (as2(kvs[:, 3, :]), P), (small[:, :, :], 16)])

            def a_pe(pe, t, S):
                if t.i >= 9:
                    turn_s(pe, t.i - 9, t.n - 1, S)
                return full(pe, t, S)

            def a_evac(dve, t, S):
                bank = G[t.slot()]
                if t.i < 4:
                    return dve.tensor_scalar(q4[:, t.i, :], bank[:, 0:T2], SCALE2, None, ALU.mult)
                if t.i < 6:
                    return dve.tensor_copy(kvc[:, t.i - 4, 0:T2], bank[:, 0:T2])
                if t.i < 8:
                    return dve.tensor_copy(kvs[:, t.i - 6, :], bank[:, 0:T2])
                return lay_s(dve, t, S)

            def a_act(act, t, S):
                if t.i >= 9:
                    copy_s(act, t.i - 9, S)

            gemm_flat("a_proj", n, n + 11, base, total, a_pe, a_evac, a_act, sems=("turned", "copied"),
                      pe_end=lambda pe, S: turn_s(pe, 2, n + 10, S), act_end=lambda act, S: copy_s(act, 2, S))
            n += 11

            with Phase("blocks") as ph:
                padded = ph.sem("padded")
                summed = ph.sem("summed")
                high = ph.sem("high")
                low = ph.sem("low")
                gated = ph.sem("gated")
                fx = ph.sem("fx")
                fe = ph.sem("fe")
                fl_ = ph.sem("fl")
                lm = ph.sem("lm")

                @ph.block.sync
                def _(sp):
                    clear_old(sp)

                @ph.block.scalar
                def _(act):
                    act.activation(gates[:, :, :], small[:, :, 0:12], ACT.Sigmoid).then_inc(gated, 1)
                    act.wait_ge(fx, 2)
                    act.activation(flog[:, 1, :], flog[:, 1, :], ACT.Exp, scale=-1.0).then_inc(fe, 1)
                    act.wait_ge(fe, 1)
                    act.activation(flog[:, 1, :], flog[:, 1, :], ACT.Ln, bias=1.0).then_inc(fe, 1)
                    act.wait_ge(lm, 2)
                    act.activation(lamb[:, 2:4], A[0][:, 0:2], ACT.Exp).then_inc(lm, 1)

                @ph.block.tensor
                def _(pe):
                    pe.wait_ge(lm, 1)
                    pe.matmul(A[0][:, 0:2], cst("ones", 128), lamb[:, 0:2], start=True, stop=True).then_inc(lm, 1)

                @ph.block.vector
                def _(dve):
                    dve.memset(kvc[:, :, T2:T1], 0.0).then_inc(padded, 1)
                    dve.memset(tbh[:, :, 512:BW].bitcast(F32), 0.0)
                    dve.memset(tbl[:, :, 512:BW].bitcast(F32), 0.0)
                    dve.memset(hidh[:, :, :].bitcast(F32), 0.0)
                    dve.memset(hidl[:, :, :].bitcast(F32), 0.0)
                    dve.wait_ge(padded, 1)
                    for a, pe_name in enumerate(("pe_k", "pe_v")):
                        if a:
                            dve.wait_ge(low, 1)
                        src = kvc[:, a, :]
                        win = bass.AP(src.tensor, src.offset, [list(src.ap[0]), [1, 32], [16, CMPW]])
                        posn = v2[:, V2[pe_name]:V2[pe_name] + 32].unsqueeze(2).to_broadcast([P, 32, CMPW])
                        dve.tensor_tensor(tb[:, :].rearrange("p (j c) -> p j c", j=32), win, posn, ALU.add).then_inc(summed, 1)
                        dve.wait_ge(summed, a + 1)
                        dve.tensor_scalar(tbh[:, a, 0:512], tb[:, :], 1.0, None, ALU.mult).then_inc(high, 1)
                        dve.wait_ge(high, a + 1)
                        dve.tensor_tensor(tbl[:, a, 0:512], tb[:, :], tbh[:, a, 0:512].bitcast(F32), ALU.subtract).then_inc(low, 1)
                    f0, f1, f2 = (flog[:, k, :] for k in range(3))
                    v_ = lambda x: x.rearrange("p (a h) -> p a h", a=2)
                    dve.tensor_tensor(v_(f0), small[:, :, 12:16],
                                      v2[:, V2["forget"]:V2["forget"] + 4].unsqueeze(1).to_broadcast([P, 2, 4]), ALU.add).then_inc(fx, 1)
                    dve.wait_ge(fx, 1)
                    dve.scalar_tensor_tensor(out=f1, in0=f0, scalar=-1.0, in1=f0, op0=ALU.mult, op1=ALU.max).then_inc(fx, 1)
                    dve.tensor_scalar(f2, f0, -1.0, 0.0, ALU.mult, ALU.max).then_inc(fx, 1)
                    dve.wait_ge(fe, 2)
                    dve.wait_ge(fx, 3)
                    dve.tensor_tensor(f0, f1, f2, ALU.add)
                    lam = v2[:, V2["lam"]:V2["lam"] + 4].rearrange("p (a e) -> p a e", a=2)
                    dve.tensor_tensor(lamb[:, 0:2].unsqueeze(2), lam[:, :, 0:1], lam[:, :, 1:2], ALU.mult).then_inc(lm, 1)
                    dve.wait_ge(lm, 3)
                    dve.tensor_tensor(lamb[:, 4:5], lamb[:, 3:4], lamb[:, 2:3], ALU.subtract).then_inc(lm, 1)
                    dve.wait_ge(lm, 4)
                    dve.tensor_tensor(lamb[:, 5:6], lamb[:, 4:5], v2[:, V2["lam_init"]:V2["lam_init"] + 1], ALU.subtract)

            def c_pe(pe, t, S):
                if t.i in (4, 8):
                    a = t.i // 4 - 1
                    pe.wait_ge(S["hidden"], a + 1)
                    for hc in range(2):
                        m = pe.transpose(A[2 + a][:, hc * CMPW:(hc + 1) * CMPW], hidg[:, a, hc * P:(hc + 1) * P],
                                         cst("ident", CMPW)[0:CMPW])
                    m.then_inc(S["hidden_t"], 1)
                if t.i < 8:
                    a, m = divmod(t.i, 4)
                    window = lambda j: slice((8 * m + j) * CMPW, (8 * m + j) * CMPW + P)
                    return product(pe, A[a][:, 0:256], lambda j: (tbh[:, a, window(j)], tbl[:, a, window(j)]),
                                   lambda j: weights(t, j * 256, 256), 8, start=(m == 0), stop=(m == 3))
                pe.wait_ge(S["hidden_lo"], 2)
                bank = G[t.slot()]
                product(pe, bank[:, 0:CMPW], lambda hc: weights(t, hc * 256, P),
                        lambda hc: (hidh[:, hc, 0:CMPW], hidl[:, hc, 0:CMPW]), 2)
                return product(pe, bank[:, 128:256], lambda hc: (hidh[:, 2 + hc, :], hidl[:, 2 + hc, :]),
                               lambda hc: weights(t, hc * 256 + P, P), 2)

            def c_act(act, t, S):
                if t.i in (3, 7):
                    a = t.i // 4
                    act.wait_ge(w_used, t.n + 1)
                    act.activation(hidg[:, a, :], A[a][0:CMPW, 0:256], ACT.Gelu_apprx_tanh).then_inc(S["hidden"], 1)

            def c_evac(dve, t, S):
                if t.i in (3, 7):
                    a = t.i // 4
                    turned = A[2 + a][:, 0:2 * CMPW].rearrange("p (e c) -> p e c", e=2)
                    dve.wait_ge(S["hidden_t"], a + 1)
                    dve.tensor_scalar(hidh[:, 2 * a:2 * a + 2, 0:CMPW], turned, 1.0, None, ALU.mult).then_inc(S["hidden_hi"], 1)
                    dve.wait_ge(S["hidden_hi"], a + 1)
                    dve.tensor_tensor(hidl[:, 2 * a:2 * a + 2, 0:CMPW], turned,
                                      hidh[:, 2 * a:2 * a + 2, 0:CMPW].bitcast(F32), ALU.subtract).then_inc(S["hidden_lo"], 1)
                if t.i == 8:
                    dve.tensor_copy(kcmp[:, :], G[t.slot()][:, 0:CMPW])
                    return dve.tensor_copy(vcmp[:, :], G[t.slot()][0:CMPW, 128:256])

            gemm_flat("a_cmp", n, n + 9, base, total, c_pe, c_evac, c_act, sems=("hidden", "hidden_t", "hidden_hi", "hidden_lo"))
            n += 9
            rope("a_rope", [q4[:, c, :] for c in range(4)] + [kvs[:, 0, :], kvs[:, 1, :]], T2, cst("rot_h", 128),
                 cst("cos_h", T2), cst("sin_h", T2), R_S, dests=[qr[:, c, :] for c in range(4)] + [kvs[:, 0, :], kvs[:, 1, :]])

            def into_parts(mixer):
                def act_(act, g, bank, u, valued, v):
                    act.wait_ge(valued, v)
                    return act.activation(fh2[:, 4 * mixer + u["h"], u["q0"]:u["q0"] + P], bank[:, 0:P], ACT.Copy)

                def dve_(dve, g, bank, u, taken_hi, valued, v):
                    dve.wait_ge(taken_hi, g + 1)
                    at = (slice(None), 4 * mixer + u["h"], slice(u["q0"], u["q0"] + P))
                    return dve.tensor_tensor(fl2[at], bank[:, 0:P], fh2[at].bitcast(F32), ALU.subtract)
                return dict(act=act_, dve=dve_)

            causal = lambda i: cst("causal", 256)[:, (1 - i) * P:256]
            key_tiles = lambda i: [(0, P), (P, P)][:i + 1]
            units = []
            for h in range(4):
                for i in range(2):
                    q = slice(i * P, (i + 1) * P)
                    nk = (i + 1) * P
                    common = dict(nq=P, h=h, q0=i * P, group=2 * h + i)
                    units.append(dict(scores=[(q4[:, h, q], kcmp[:, :], 0)], nk=CMPW,
                                      mask=cst("cmp", 32)[:, i * CMPW:(i + 1) * CMPW], keys=[(0, CMPW)],
                                      values=[vcmp[:, :]], factor=gates[:, i, 3 * h:3 * h + 1],
                                      valid=cst("cmp01", 32)[:, i * CMPW:i * CMPW + 1], first=True, last=False, **common))
                    for j in range(2):
                        vals = kvs[:, 2 + j, :].rearrange("p (a d) -> p a d", a=2)
                        units.append(dict(scores=[(qr[:, h, q], kvs[:, j, 0:nk], 0)], nk=nk, mask=causal(i),
                                          keys=key_tiles(i), values=[vals[:, k, :] for k in range(i + 1)],
                                          factor=gates[:, i, 3 * h + 1 + j:3 * h + 2 + j], first=False, last=(j == 1),
                                          **common))
            attention("a_attn", units, 8, into_parts(0), R_S)
            if stop == "a":
                return

            lay_v, turn_v, copy_v = turning(8, [(v4[:, :, h * P:(h + 1) * P], P) for h in range(4)])

            def qkv(name, n, scale):
                def pe_tile(pe, t, S):
                    if t.i >= 9:
                        turn_v(pe, t.i - 9, t.n - 1, S)
                    return full(pe, t, S)

                def evac(dve, t, S):
                    bank = G[t.slot()]
                    if t.i < 4:
                        return dve.tensor_scalar(q4[:, t.i, :], bank[:, 0:T2], scale, None, ALU.mult)
                    if t.i < 8:
                        return dve.tensor_copy(k4[:, t.i - 4, :], bank[:, 0:T2])
                    return lay_v(dve, t, S)

                def act_tile(act, t, S):
                    if t.i >= 9:
                        copy_v(act, t.i - 9, S)

                gemm_flat(name, n, n + 12, base, total, pe_tile, evac, act_tile, sems=("turned", "copied"),
                          pe_end=lambda pe, S: turn_v(pe, 3, n + 11, S), act_end=lambda act, S: copy_v(act, 3, S))

            qkv("b_proj", n, SCALE2)
            n += 12
            stick("b_attn", into=1)
            qkv("c_proj", n, SCALE2)
            n += 12
            units = []
            for h in range(4):
                for i in range(2):
                    q = slice(i * P, (i + 1) * P)
                    nk = (i + 1) * P
                    scores = [(q4[:, h, q], k4[:, h, 0:nk], 0)]
                    for k in range(i + 1):
                        scores.append((flog[:, 0, 4 * k + h:4 * k + h + 1].to_broadcast([P, P]),
                                       cst("tri_le", 256)[:, 0:nk - k * P], k * P))
                    units.append(dict(scores=scores, nq=P, nk=nk, mask=causal(i), keys=key_tiles(i),
                                      values=[v4[:, k, h * P:(h + 1) * P] for k in range(i + 1)], factor=None,
                                      group=len(units), first=True, last=True, h=h, q0=i * P))
            attention("c_attn", units, 8, into_parts(2), R_S)
            qkv("d_proj", n, SCALE_DIFF)
            n += 12
            rope("d_rope", [q4[:, c, :] for c in range(4)] + [k4[:, c, :] for c in range(4)], T2, cst("rot_d", 128),
                 cst("cos_d", T2), cst("sin_d", T2), R_S)
            units = []
            for h in range(4):
                for i in range(2):
                    nk = (i + 1) * P
                    for j in range(2):
                        half = slice(64 * j, 64 * j + 64)
                        units.append(dict(scores=[(q4[half, h, i * P:(i + 1) * P], k4[half, h, 0:nk], 0)], nq=P, nk=nk,
                                          mask=causal(i), keys=key_tiles(i),
                                          values=[v4[:, k, h * P:(h + 1) * P] for k in range(i + 1)],
                                          factor=None if j == 0 else lamb[:, 5:6], group=2 * h + i, first=(j == 0),
                                          last=(j == 1), h=h, q0=i * P))

            def out_d(dve, g, bank, u, taken_hi, valued, v):
                dve.wait_ge(valued, v)
                return dve.tensor_copy(qr[:, u["h"], u["q0"]:u["q0"] + P], bank[:, 0:P])

            attention("d_attn", units, 8, dict(dve=out_d), R_S)
            with Phase("d_norm") as ph:
                od = qr[:, :, :].rearrange("p h t -> p (h t)")
                sq = q4[:, :, :].rearrange("p h t -> p (h t)")
                squared, summed, rooted, chain, high, low = (ph.sem(k) for k in ("squared", "summed", "rooted", "chain", "high", "low"))
                gain = lamb[:, 6:7]
                o12 = slice(12, 16)

                @ph.block.sync
                def _(sp):
                    clear_old(sp)

                @ph.block.scalar
                def _(act):
                    act.activation(sq, od, ACT.Square).then_inc(squared, 1)
                    for k in range(2):
                        act.wait_ge(summed, k + 1)
                        act.activation(sq[:, 512 * k:512 * k + 512], A[k][:, :], ACT.Sqrt, bias=eps[:, 0:1],
                                       scale=1.0 / 128).then_inc(rooted, 1)
                    act.wait_ge(chain, 3)
                    act.activation(fh2[:, o12, :], qr[:, :, :], ACT.Copy).then_inc(high, 1)

                @ph.block.tensor
                def _(pe):
                    pe.wait_ge(squared, 1)
                    for k in range(2):
                        pe.matmul(A[k][:, :], cst("ones", 128), sq[:, 512 * k:512 * k + 512], start=True, stop=True).then_inc(summed, 1)

                @ph.block.vector
                def _(dve):
                    dve.tensor_tensor(gain, g2("diff_norm")(0), v2[:, V2["one_less_init"]:V2["one_less_init"] + 1],
                                      ALU.mult).then_inc(chain, 1)
                    dve.wait_ge(rooted, 2)
                    dve.reciprocal(sq, sq).then_inc(chain, 1)
                    dve.wait_ge(chain, 2)
                    dve.scalar_tensor_tensor(out=od, in0=od, scalar=gain, in1=sq, op0=ALU.mult, op1=ALU.mult).then_inc(chain, 1)
                    dve.wait_ge(high, 1)
                    dve.tensor_tensor(fl2[:, o12, :], qr[:, :, :], fh2[:, o12, :].bitcast(F32), ALU.subtract)
            if stop == "mixers":
                return

            def set_chunk(dve, t, S):
                return dve.tensor_scalar(chunk_of(y2)(t.i), G[t.slot()][:, 0:T2], 1.0, None, ALU.mult)

            gemm("w_out2", n, n + 16, base, total, full_tile(fh2, fl2, T2), set_chunk)
            n += 16
            rms_norm("mix_post", lambda c: y2[:, c, :], g2("mix_post"), DC, T2, D, add=X)
            if stop == "xa":
                return
            rms_norm("mlp_pre", X, g2("mlp_pre"), DC, T2, D, hi=lambda c: xh2[:, c, :], lo=lambda c: xl2[:, c, :])
            n = feed_forward("ffn2", n, PASSES2, T2, xh2, xl2, fh2, fl2, v2, V2, True, False,
                             lambda p: set_chunk if p == 0 else add_chunk(chunk_of(y2), T2), base, total)
            assert n == N2, (n, N2)
            rms_norm("mlp_post", lambda c: y2[:, c, :], g2("mlp_post"), DC, T2, D, add=X)

        def gemm_flat(*a, **k):
            return gemm(*a, **k, flat=True)

        def stick(name, into):
            W = 384
            with Phase(name) as ph:
                B0 = R_S
                ab = b.at("abs_z", [P, 2, W], B0)
                sp_ = b.at("softplus", [P, 2, W], B0 + 3072)
                zm = b.at("z_masked", [P, 2, W], B0 + 6144)
                scored, absd, logd, plus, masked, zmd, summed, arg, weighed, valued, high, taken = (
                    ph.sem(k) for k in ("scored", "absd", "logd", "plus", "masked", "zmd", "summed", "arg", "weighed",
                                        "valued", "high", "taken"))
                H = 4

                @ph.block.sync
                def _(sp):
                    clear_old(sp)

                @ph.block.tensor
                def _(pe):
                    def scores(h):
                        if h >= 2:
                            pe.wait_ge(zmd, h - 1)
                        bank = A[h % 2]
                        pe.matmul(bank[:, 0:256], k4[:, h, 0:P], q4[:, h, :], start=True, stop=True)
                        pe.matmul(bank[:, 256:W], k4[:, h, P:T2], q4[:, h, P:T2], start=True, stop=True).then_inc(scored, 1)

                    def sums(h):
                        pe.wait_ge(masked, h + 1)
                        if h >= 2:
                            pe.wait_ge(arg, h - 1)
                        bank = A[2 + h % 2]
                        s = sp_[:, h % 2, :]
                        pe.matmul(bank[:, 0:256], cst("tri_ge", P), s[:, 0:256], start=True, stop=False, skip_group_check=True)
                        pe.matmul(bank[:, 128:256], cst("ones", P), s[:, 256:W], start=False, stop=True, skip_group_check=True)
                        pe.matmul(bank[:, 256:W], cst("tri_ge", P), s[:, 256:W], start=True, stop=True).then_inc(summed, 1)

                    def value(h):
                        pe.wait_ge(weighed, h + 1)
                        if h >= 2:
                            pe.wait_ge(taken, h - 1)
                        bank = G[h % 2]
                        pe.matmul(bank[:, 0:256], v4[:, 0, h * P:(h + 1) * P], zm[:, h % 2, 0:256], start=True, stop=False,
                                  skip_group_check=True)
                        pe.matmul(bank[:, 128:256], v4[:, 1, h * P:(h + 1) * P], zm[:, h % 2, 256:W], start=False, stop=True,
                                  skip_group_check=True).then_inc(valued, 1)

                    scores(0)
                    for h in range(H):
                        if h + 1 < H:
                            scores(h + 1)
                        sums(h)
                        value(h)

                @ph.block.scalar
                def _(act):
                    def logs(h):
                        z = A[h % 2][:, 0:W]
                        a = ab[:, h % 2, :]
                        act.wait_ge(scored, h + 1)
                        if h >= 2:
                            act.wait_ge(plus, h - 1)
                        act.activation(a, z, ACT.Abs).then_inc(absd, 1)
                        act.wait_ge(absd, 2 * h + 1)
                        act.activation(a, a, ACT.Exp, scale=-1.0).then_inc(absd, 1)
                        act.wait_ge(absd, 2 * h + 2)
                        act.activation(a, a, ACT.Ln, bias=1.0).then_inc(logd, 1)

                    def weigh(h):
                        act.wait_ge(arg, h + 1)
                        act.activation(zm[:, h % 2, :], zm[:, h % 2, :], ACT.Exp).then_inc(weighed, 1)
                        act.wait_ge(valued, h + 1)
                        act.activation(fh2[:, 4 * into + h, :], G[h % 2][:, 0:T2], ACT.Copy).then_inc(high, 1)

                    logs(0)
                    for h in range(H):
                        if h + 1 < H:
                            logs(h + 1)
                        weigh(h)

                @ph.block.vector
                def _(dve):
                    def soft(h):
                        z = A[h % 2][:, 0:W]
                        s = sp_[:, h % 2, :]
                        dve.wait_ge(logd, h + 1)
                        if h >= 2:
                            dve.wait_ge(summed, h - 1)
                        dve.scalar_tensor_tensor(out=s, in0=z, scalar=0.0, in1=ab[:, h % 2, :], op0=ALU.max, op1=ALU.add).then_inc(plus, 1)
                        dve.wait_ge(plus, h + 1)
                        dve.tensor_tensor(s, s, cst("past", W), ALU.mult).then_inc(masked, 1)
                        if h >= 2:
                            dve.wait_ge(valued, h - 1)
                        dve.tensor_tensor(zm[:, h % 2, :], z, cst("past_neg", W), ALU.add).then_inc(zmd, 1)

                    def finish(h):
                        dve.wait_ge(summed, h + 1)
                        dve.wait_ge(zmd, h + 1)
                        dve.tensor_tensor(zm[:, h % 2, :], zm[:, h % 2, :], A[2 + h % 2][:, 0:W], ALU.subtract).then_inc(arg, 1)
                        dve.wait_ge(high, h + 1)
                        dve.tensor_tensor(fl2[:, 4 * into + h, :], G[h % 2][:, 0:T2], fh2[:, 4 * into + h, :].bitcast(F32),
                                          ALU.subtract).then_inc(taken, 1)

                    soft(0)
                    for h in range(H):
                        if h + 1 < H:
                            soft(h + 1)
                        finish(h)

        flush(stream_sems)
        if upto is None:
            with nc.Fori(0, LAYERS) as l:
                layer(l, l * N2 + N1)
                flush(stream_sems)
        else:
            stop = upto
            layer(0, N1, stop)
            if stop == "a":
                dump([(dbg[0], fh2[:, 0:4, :].bitcast(F32))])
            elif stop == "mixers":
                dump([(dbg[0], fh2[:, :, :].bitcast(F32))])
            else:
                dump([(dbg[0], xT[:, :, :])])
            return
        with Phase("store") as ph:
            stored = ph.sem("stored")

            @ph.block.sync
            def _(sp):
                sp.dma_start(outs, xT[:, :, META:T1]).then_inc(stored, 16)
                sp.wait_ge(stored, 16)



def _pack(w, rows, cols):
    k = [w[r:r + P][:, cols] for r in rows]
    t = np.concatenate(k, axis=1)
    if t.shape[1] < TILE:
        t = np.concatenate([t, np.zeros((P, TILE - t.shape[1]), t.dtype)], axis=1)
    return t


def _cols(w, first, count, width=P, nk=DC):
    rows = [k * P for k in range(nk)]
    return [_pack(w, rows, slice(first + width * c, first + width * (c + 1))) for c in range(count)]


def _ffn(up, down, half, passes):
    out, off = [], 0
    for np_ in passes:
        for j in range(off, off + np_):
            out += _cols(up, j * P, 1) + _cols(up, half + j * P, 1)
        for c in range(DC):
            out.append(_pack(down, [(off + k) * P for k in range(np_)], slice(c * P, c * P + P)))
        off += np_
    return out


def _vec(a):
    return a.reshape(-1, P).T


def lay_out(x):
    first, second = [], []
    w = x["w_in"][0]
    first += _cols(w, 0, 8)
    first += [_pack(np.concatenate([w[:, 1792:1856]] * 2, axis=1), [k * P for k in range(DC)], slice(0, P))]
    first += _cols(w, 1024, 6)
    q = x["w_q_b"][0].reshape(512, 8, 192)
    q = np.concatenate([q[:, :, :128].reshape(512, 1024), q[:, :, 128:].reshape(512, 512)], axis=1)
    first += _cols(q, 0, 3, 512, 4)
    kv = x["w_kv_b"][0].reshape(256, 8, 256)
    kv = np.concatenate([kv[:, :, :128].reshape(256, 1024), kv[:, :, 128:].reshape(256, 1024)], axis=1)
    first += _cols(kv, 0, 2, 1024, 2)
    first += _cols(x["w_glu"][0], 0, 4, 256, 8)
    first += _cols(x["w_out"][0], 0, 16)
    first += _ffn(x["w_up"][0], x["w_down"][0], FF1, PASSES1)
    assert len(first) == N1
    for l in range(LAYERS):
        w = x["w_in_2"][l]
        t = []
        small = np.concatenate([w[:, 1280:1292], w[:, 4364:4368]], axis=1)
        t += _cols(w, 0, 4) + _cols(w, 512, 1) + _cols(w, 640, 1) + _cols(w, 768, 1) + _cols(w, 1024, 1)
        t += _cols(w, 896, 1) + _cols(w, 1152, 1)
        t += _cols(np.concatenate([small, np.zeros((D, P - 16), small.dtype)], axis=1), 0, 1)
        for name in ("k", "v"):
            c = x[f"nsa_cmp_{name}1_2"][l]
            for m in range(4):
                t.append(_pack(c, [(8 * m + j) * P for j in range(8)], slice(0, 256)))
        t.append(_pack(np.concatenate([x["nsa_cmp_k2_2"][l], x["nsa_cmp_v2_2"][l]], axis=1), [0, P], slice(0, 256)))
        for at in (1292, 2828, 4368):
            t += _cols(w, at, 12)
        t += _cols(x["w_out_2"][l], 0, 16)
        t += _ffn(x["mlp_w_up_2"][l], x["mlp_w_down_2"][l], FF2, PASSES2)
        assert len(t) == N2
        second += t
    stream = np.stack(first + second)
    h = np.concatenate([x["meta_tokens"], x["x"][0]], axis=0)
    out = {"stream": stream, "hT": np.ascontiguousarray(h.T.reshape(DC, P, T1).transpose(1, 0, 2)).reshape(P, DC * T1)}
    out["vec1"] = np.concatenate([_vec(x[k][0] if x[k].ndim == 2 else x[k]) for k in
                                  ("mix_norm", "ffn_norm", "final_norm", "out_norm_ssm", "out_norm_attn", "q_a_norm",
                                   "kv_a_norm", "d_skip", "b_glu")] +
                                 [_vec(x["conv_w"][0][k]) for k in range(3)] + [_vec(x["conv_b"][0])], axis=1)
    s5 = [x[k][0].reshape(PAIRS, P).T for k in ("lam_re", "lam_im")]
    s5.append(np.repeat(x["log_dt"][0].reshape(PAIRS, 2), 64, axis=1).T)
    for k in ("b_re", "b_im", "c_re", "c_im"):
        m = x[k][0] if k[0] == "b" else x[k][0].transpose(0, 2, 1)
        wide = np.zeros((2, 64, PAIRS, 2, 16), m.dtype)
        for g in range(2):
            wide[g, :, :, g, :] = m.reshape(PAIRS, 2, 64, 16)[:, g].transpose(1, 0, 2)
        s5.append(wide.reshape(P, PAIRS * 32))
    out["s5"] = np.concatenate(s5, axis=1)
    vec2 = []
    for l in range(LAYERS):
        v = [_vec(x[f"norm_{k}_2"][l]) for k in ("mix_pre", "mix_post", "mlp_pre", "mlp_post")]
        v.append(_vec(x["diff_norm_2"][l]))
        v += [x[f"nsa_pe_{k}_2"][l].T for k in "kv"]
        v += [_vec(x["mlp_conv_w_2"][l][k]) for k in range(3)] + [_vec(x["mlp_conv_b_2"][l])]
        v.append(np.broadcast_to(x["fox_forget_bias_2"][l], (P, 4)))
        lam = np.zeros((P, 4), x["diff_lambda_2"].dtype)
        lam[0:64] = x["diff_lambda_2"][l].T
        v.append(lam)
        init = 0.8 - 0.6 * math.exp(-0.3 * l)
        v.append(np.full((P, 1), init, np.float32))
        v.append(np.full((P, 1), 1.0 - init, np.float32))
        vec2.append(np.concatenate(v, axis=1))
    out["vec2"] = np.stack(vec2)
    out["const1"], out["const2"] = constants()
    return {k: np.ascontiguousarray(v) for k, v in out.items()}


def _swap(block, half):
    r = np.zeros((P, P), np.float32)
    for b0 in range(0, P, block):
        for i in range(half):
            r[b0 + i + half, b0 + i] = -1.0
            r[b0 + i, b0 + i + half] = 1.0
    return r


def _tables(positions, inv, block):
    ang = (positions[:, None].astype(np.float32) * inv[None, :].astype(np.float32)).astype(np.float32)
    cos, sin = np.ones((P, len(positions)), np.float32), np.zeros((P, len(positions)), np.float32)
    half = len(inv)
    for b0 in range(0, P, block):
        for k in (0, half):
            cos[b0 + k:b0 + k + half] = np.cos(ang).T
            sin[b0 + k:b0 + k + half] = np.sin(ang).T
    return cos, sin


def constants():
    f = np.float32
    eye, ones = np.eye(P, dtype=f), np.ones((P, P), f)
    pos = np.arange(T1)
    chunk = np.where(pos < META, 0, 1 + (pos - META) // 64)
    inv = (f(1.0) / (f(10000.0) ** (np.arange(0, ROPE1, 2, dtype=f) / f(ROPE1)))).astype(f)
    cos, sin = _tables(pos, inv, 64)
    masks = []
    for (q0, nq), nk in list(zip(QT1, KEYS1))[:2]:
        m = np.zeros((P, nk), f)
        m[:nq] = np.where(chunk[None, :nk] <= chunk[q0:q0 + nq, None], 0, NEG)
        masks.append(m)
    c1 = np.concatenate([eye, ones, _swap(64, 32), cos, sin, *masks, np.zeros((P, T1), f)], axis=1)
    assert c1.shape[1] == NC1
    pos = np.arange(T2)
    i, j = np.arange(P)[:, None], np.arange(P)[None, :]
    tab = []
    for rot, block in ((32, 128), (16, 64)):
        inv = (f(500000.0) ** (-np.arange(0, rot, 2, dtype=f) / f(rot))).astype(f)
        tab += _tables(pos, inv, block)
    causal = np.concatenate([np.zeros((P, P), f), np.where(j <= i, 0, NEG).astype(f)], axis=1)
    tri_ge = (i >= j).astype(f)
    tri_le = np.concatenate([(i <= j).astype(f), ones], axis=1)
    past = np.concatenate([(i < j).astype(f), ones, (i < j).astype(f)], axis=1)
    past_neg = np.where(past > 0, 0, NEG).astype(f)
    ends = np.arange(CMPW) * 16 + 31
    valid = np.stack([(ends[None, :] <= (t0 + i)) & (np.arange(CMPW)[None, :] < NCMP) for t0 in (0, P)], axis=1)
    cmp_neg = np.where(valid, 0, NEG).astype(f).reshape(P, 32)
    cmp_neg.reshape(P, 2, CMPW)[:, :, NCMP] = 3 * NEG
    c2 = np.concatenate([eye, ones, _swap(128, 16), _swap(64, 8), *tab, causal, tri_ge, tri_le, past, past_neg, cmp_neg,
                         valid.astype(f).reshape(P, 32)], axis=1)
    assert c2.shape[1] == NC2
    return c1, c2


_SHAPES = dict(stream=(N1 + LAYERS * N2, P, TILE), hT=(P, DC * T1), vec1=(P, NV1), s5=(P, 96 + 4096),
               vec2=(LAYERS, P, NV2), const1=(P, NC1), const2=(P, NC2))


def kernel(**inputs):
    import concourse.bacc as bacc
    from concourse.bass_utils import run_bass_kernel_spmd

    laid = lay_out({k: np.asarray(v) for k, v in inputs.items()})
    nc = bacc.Bacc("TRN2", target_bir_lowering=False, num_devices=1)
    arrays, ins = {}, {}
    for name, a in laid.items():
        assert a.shape == _SHAPES[name]
        arrays[f"in_{name}_dram"] = a
        ins[name] = nc.dram_tensor(f"in_{name}_dram", a.shape, mybir.dt.from_np(a.dtype), kind="ExternalInput").ap()
    out = nc.dram_tensor("out_0_dram", (P, DC, T2), F32, kind="ExternalOutput").ap()
    build(nc, ins, out)
    r = run_bass_kernel_spmd(nc, [arrays], core_ids=[0])
    got = r.results[0]["out_0_dram"]
    return got.transpose(2, 1, 0).reshape(1, T2, D)
```
